# Optimizing a Trainium2 kernel written in Bass

```python
import jax, jax.numpy as jnp
from jax import lax
import numpy as np

D_MODEL = 1024
BATCH = 1
SEQ = 512
DEPTH = 2

HEAD_DIM = 64
EPS = 1e-6
N_BRANCH = 3
CONV_WIDTH = D_MODEL
CONV_KERNEL = 31
RET_HEADS = 4
RET_QK_DIM = D_MODEL // RET_HEADS
RET_V_DIM = 2 * RET_QK_DIM
RET_CHUNK = 128
RET_THETA = 10000.0
ATTN_HEADS = D_MODEL // HEAD_DIM
ATTN_KV_HEADS = 4
ATTN_WINDOW = 128
ATTN_BLOCK = 128
ROPE_THETA = 500000.0
ROPE_DIM = HEAD_DIM // 4

IN_SPLITS = (
    2 * CONV_WIDTH,
    CONV_WIDTH,
    RET_HEADS * RET_QK_DIM,
    RET_HEADS * RET_QK_DIM,
    RET_HEADS * RET_V_DIM,
    RET_HEADS * RET_V_DIM,
    ATTN_HEADS * HEAD_DIM,
    ATTN_KV_HEADS * HEAD_DIM,
    ATTN_KV_HEADS * HEAD_DIM,
    ATTN_HEADS * HEAD_DIM,
    N_BRANCH * D_MODEL,
)
IN_WIDTH = sum(IN_SPLITS)


def rms_norm(x, g):
    xf = x.astype(jnp.float32)
    y = xf * lax.rsqrt(jnp.mean(xf * xf, axis=-1, keepdims=True) + EPS) * g.astype(jnp.float32)
    return y.astype(x.dtype)

def rotary(x, positions, theta, rot_dim):
    half = rot_dim // 2
    inv_freq = theta ** (-jnp.arange(half, dtype=jnp.float32) / half)
    ang = positions.astype(jnp.float32)[:, None] * inv_freq[None, :]
    cos = jnp.cos(ang)[:, None, :]
    sin = jnp.sin(ang)[:, None, :]
    xf = x.astype(jnp.float32)
    x1 = xf[..., :half]
    x2 = xf[..., half:rot_dim]
    out = jnp.concatenate([x1 * cos - x2 * sin, x2 * cos + x1 * sin, xf[..., rot_dim:]], axis=-1)
    return out.astype(x.dtype)

def conv_module(u_glu, gate, dw, db, ln_g, ln_b):
    a, b = jnp.split(u_glu, 2, axis=-1)
    v = a * jax.nn.sigmoid(b)
    y = lax.conv_general_dilated(
        v, dw[:, None, :].astype(v.dtype), window_strides=(1,),
        padding=[(CONV_KERNEL // 2, CONV_KERNEL // 2)],
        dimension_numbers=('NWC', 'WIO', 'NWC'),
        feature_group_count=CONV_WIDTH) + db.astype(v.dtype)
    yf = y.astype(jnp.float32)
    mu = jnp.mean(yf, axis=-1, keepdims=True)
    var = jnp.mean(jnp.square(yf - mu), axis=-1, keepdims=True)
    yf = (yf - mu) * lax.rsqrt(var + EPS) * ln_g.astype(jnp.float32) + ln_b.astype(jnp.float32)
    y = jax.nn.silu(yf).astype(v.dtype)
    return y * jax.nn.silu(gate)

def retention_one_direction(q, k, v, log_gamma, inclusive):
    B, H, S, dk = q.shape
    dv = v.shape[-1]
    C = RET_CHUNK
    n = S // C
    qc = q.reshape(B, H, n, C, dk)
    kc = k.reshape(B, H, n, C, dk)
    vc = v.reshape(B, H, n, C, dv)
    idx = jnp.arange(C, dtype=jnp.float32)
    diff = idx[:, None] - idx[None, :]
    mask = (diff >= 0) if inclusive else (diff > 0)
    lg = log_gamma[:, None, None]
    decay_inner = jnp.where(mask[None], jnp.exp(lg * jnp.where(mask, diff, 0.0)[None]), 0.0)
    scores = jnp.einsum('bhnid,bhnjd->bhnij', qc, kc) * decay_inner[None, :, None]
    inner = jnp.einsum('bhnij,bhnjv->bhniv', scores, vc)
    q_decay = jnp.exp(log_gamma[:, None] * (idx[None, :] + 1.0))[None, :, :, None]
    k_decay = jnp.exp(log_gamma[:, None] * (C - 1.0 - idx[None, :]))[None, :, :, None]
    chunk_decay = jnp.exp(log_gamma * C)[None, :, None, None]

    def step(state, xs):
        q_t, k_t, v_t = xs
        cross = jnp.einsum('bhcd,bhdv->bhcv', q_t * q_decay, state)
        state = chunk_decay * state + jnp.einsum('bhcd,bhcv->bhdv', k_t * k_decay, v_t)
        return state, cross

    state0 = jnp.zeros((B, H, dk, dv), jnp.float32)
    xs = (jnp.moveaxis(qc, 2, 0), jnp.moveaxis(kc, 2, 0), jnp.moveaxis(vc, 2, 0))
    _, cross = lax.scan(step, state0, xs)
    out = inner + jnp.moveaxis(cross, 0, 2)
    return out.reshape(B, H, S, dv)

def retention_branch(q, k, v, gate, ret_decay, positions):
    B, S, _ = q.shape
    q = rotary(q.reshape(B, S, RET_HEADS, RET_QK_DIM), positions, RET_THETA, RET_QK_DIM)
    k = rotary(k.reshape(B, S, RET_HEADS, RET_QK_DIM), positions, RET_THETA, RET_QK_DIM)
    qf = jnp.transpose(q, (0, 2, 1, 3)).astype(jnp.float32)
    kf = jnp.transpose(k, (0, 2, 1, 3)).astype(jnp.float32) * (RET_QK_DIM ** -0.5)
    vf = jnp.transpose(v.reshape(B, S, RET_HEADS, RET_V_DIM), (0, 2, 1, 3)).astype(jnp.float32)
    log_gamma = -jnp.exp(ret_decay.astype(jnp.float32))
    fwd = retention_one_direction(qf, kf, vf, log_gamma[0], True)
    bwd = retention_one_direction(qf[:, :, ::-1], kf[:, :, ::-1], vf[:, :, ::-1], log_gamma[1], False)[:, :, ::-1]
    o = fwd + bwd
    mu = jnp.mean(o, axis=-1, keepdims=True)
    var = jnp.mean(jnp.square(o - mu), axis=-1, keepdims=True)
    o = (o - mu) * lax.rsqrt(var + EPS)
    o = jnp.transpose(o, (0, 2, 1, 3)).reshape(B, S, RET_HEADS * RET_V_DIM).astype(gate.dtype)
    return o * jax.nn.silu(gate)

def window_attention_branch(q, k, v, gate, q_norm_g, k_norm_g, sink, positions):
    B, S, _ = q.shape
    G = ATTN_HEADS // ATTN_KV_HEADS
    T = ATTN_BLOCK
    nb = S // T
    q = rms_norm(q.reshape(B, S, ATTN_HEADS, HEAD_DIM), q_norm_g)
    k = rms_norm(k.reshape(B, S, ATTN_KV_HEADS, HEAD_DIM), k_norm_g)
    q = rotary(q, positions, ROPE_THETA, ROPE_DIM)
    k = rotary(k, positions, ROPE_THETA, ROPE_DIM)
    v = v.reshape(B, S, ATTN_KV_HEADS, HEAD_DIM)
    qb = q.reshape(B, nb, T, ATTN_KV_HEADS, G, HEAD_DIM).astype(jnp.float32)
    pad = ((0, 0), (T, T), (0, 0), (0, 0))
    kb = jnp.pad(k, pad).reshape(B, nb + 2, T, ATTN_KV_HEADS, HEAD_DIM)
    vb = jnp.pad(v, pad).reshape(B, nb + 2, T, ATTN_KV_HEADS, HEAD_DIM)
    kwin = jnp.concatenate([kb[:, :-2], kb[:, 1:-1], kb[:, 2:]], axis=2).astype(jnp.float32)
    vwin = jnp.concatenate([vb[:, :-2], vb[:, 1:-1], vb[:, 2:]], axis=2).astype(jnp.float32)
    s = jnp.einsum('bnqhgd,bnjhd->bhgnqj', qb, kwin) * (HEAD_DIM ** -0.5)
    blk = jnp.arange(nb)[:, None, None]
    qpos = blk * T + jnp.arange(T)[None, :, None]
    kpos = (blk - 1) * T + jnp.arange(3 * T)[None, None, :]
    valid = (jnp.abs(kpos - qpos) <= ATTN_WINDOW) & (kpos >= 0) & (kpos < S)
    s = jnp.where(valid, s, -1e30)
    sink_l = sink.astype(jnp.float32).reshape(ATTN_KV_HEADS, G, 1, 1, 1)
    m = jnp.maximum(jnp.max(s, axis=-1, keepdims=True), sink_l)
    p = jnp.exp(s - m)
    p = p / (jnp.sum(p, axis=-1, keepdims=True) + jnp.exp(sink_l - m))
    o = jnp.einsum('bhgnqj,bnjhd->bnqhgd', p, vwin)
    o = o.reshape(B, S, ATTN_HEADS * HEAD_DIM).astype(gate.dtype)
    return o * jax.nn.silu(gate)

def hybrid_layer(x, positions, norm_g, w_in, b_gate, conv_dw, conv_b, conv_ln_g, conv_ln_b,
                 ret_decay, q_norm_g, k_norm_g, attn_sink, w_conv_out, w_ret_out, w_attn_out, w_out):
    B, S, D = x.shape
    h = rms_norm(x, norm_g)
    z = h @ w_in
    offsets = np.cumsum(IN_SPLITS)[:-1].tolist()
    (c_glu, c_gate, r_q, r_k, r_v, r_gate, a_q, a_k, a_v, a_gate, g_logit) = jnp.split(z, offsets, axis=-1)
    y_conv = conv_module(c_glu, c_gate, conv_dw, conv_b, conv_ln_g, conv_ln_b) @ w_conv_out
    y_ret = retention_branch(r_q, r_k, r_v, r_gate, ret_decay, positions) @ w_ret_out
    y_attn = window_attention_branch(a_q, a_k, a_v, a_gate, q_norm_g, k_norm_g, attn_sink, positions) @ w_attn_out
    g = jax.nn.sigmoid(g_logit + b_gate).reshape(B, S, N_BRANCH, D)
    merged = g[:, :, 0] * y_conv + g[:, :, 1] * y_ret + g[:, :, 2] * y_attn
    return x + merged @ w_out

def first_inputs(seed: int = 0) -> dict:
    key = jax.random.key(seed)
    ks = jax.random.split(key, 18)
    nrm = jax.random.normal
    f32 = jnp.float32
    ret_base = jnp.log(-jnp.log1p(-(2.0 ** (-5.0 - jnp.arange(RET_HEADS, dtype=f32)))))
    return {
        'x': nrm(ks[0], (BATCH, SEQ, D_MODEL), f32),
        'norm_g': 1.0 + 0.02 * nrm(ks[1], (DEPTH, D_MODEL), f32),
        'w_in': nrm(ks[2], (DEPTH, D_MODEL, IN_WIDTH), f32) * D_MODEL ** -0.5,
        'b_gate': 0.1 * nrm(ks[3], (DEPTH, N_BRANCH * D_MODEL), f32),
        'conv_dw': nrm(ks[4], (DEPTH, CONV_KERNEL, CONV_WIDTH), f32) * CONV_KERNEL ** -0.5,
        'conv_b': 0.02 * nrm(ks[5], (DEPTH, CONV_WIDTH), f32),
        'conv_ln_g': 1.0 + 0.02 * nrm(ks[6], (DEPTH, CONV_WIDTH), f32),
        'conv_ln_b': 0.02 * nrm(ks[7], (DEPTH, CONV_WIDTH), f32),
        'ret_decay': ret_base + 0.05 * nrm(ks[8], (DEPTH, 2, RET_HEADS), f32),
        'q_norm_g': 1.0 + 0.02 * nrm(ks[9], (DEPTH, HEAD_DIM), f32),
        'k_norm_g': 1.0 + 0.02 * nrm(ks[10], (DEPTH, HEAD_DIM), f32),
        'attn_sink': 0.5 * nrm(ks[11], (DEPTH, ATTN_HEADS), f32),
        'w_conv_out': nrm(ks[12], (DEPTH, CONV_WIDTH, D_MODEL), f32) * CONV_WIDTH ** -0.5,
        'w_ret_out': nrm(ks[13], (DEPTH, RET_HEADS * RET_V_DIM, D_MODEL), f32) * (RET_HEADS * RET_V_DIM) ** -0.5,
        'w_attn_out': nrm(ks[14], (DEPTH, ATTN_HEADS * HEAD_DIM, D_MODEL), f32) * (ATTN_HEADS * HEAD_DIM) ** -0.5,
        'w_out': nrm(ks[15], (DEPTH, D_MODEL, D_MODEL), f32) * D_MODEL ** -0.5,
    }

def first_block(x, norm_g, w_in, b_gate, conv_dw, conv_b, conv_ln_g, conv_ln_b, ret_decay,
              q_norm_g, k_norm_g, attn_sink, w_conv_out, w_ret_out, w_attn_out, w_out):
    positions = jnp.arange(x.shape[1], dtype=jnp.int32)
    for l in range(DEPTH):
        x = hybrid_layer(x, positions, norm_g[l], w_in[l], b_gate[l], conv_dw[l], conv_b[l],
                         conv_ln_g[l], conv_ln_b[l], ret_decay[l], q_norm_g[l], k_norm_g[l],
                         attn_sink[l], w_conv_out[l], w_ret_out[l], w_attn_out[l], w_out[l])
    return x


DEPTH_2 = 1

CHUNK = 64
GM_BLOCK = 128
GM_GROUP_DIM = 128
GM_WIDTH = D_MODEL
GM_GROUPS = GM_WIDTH // GM_GROUP_DIM
HG_DK = 128
HG_DV = 128
HG_HEADS = D_MODEL // 128
HG_KWIDTH = HG_HEADS * HG_DK
HG_WIDTH = HG_HEADS * HG_DV
HG_CHUNK = 16
D_FF = -((-8 * D_MODEL) // (3 * 256)) * 256
PLE_DIM = 256
ALPHA = (2.0 * DEPTH_2) ** 0.25
BETA = (8.0 * DEPTH_2) ** -0.25
LN_EPS = 1e-5
RMS_EPS = 1e-6
IN_SPLITS_2 = (GM_WIDTH, GM_WIDTH, HG_KWIDTH, HG_KWIDTH, HG_WIDTH, HG_WIDTH, D_MODEL, D_MODEL)
D_IN = sum(IN_SPLITS_2)
IN_OFFSETS = tuple(int(o) for o in np.cumsum(IN_SPLITS_2)[:-1])


def _layer_norm(x, g, b):
    xf = x.astype(jnp.float32)
    xc = xf - jnp.mean(xf, -1, keepdims=True)
    var = jnp.mean(xc * xc, -1, keepdims=True)
    y = xc * lax.rsqrt(var + LN_EPS) * g.astype(jnp.float32) + b.astype(jnp.float32)
    return y.astype(x.dtype)

def _rms_norm(x, g):
    return x * lax.rsqrt(jnp.mean(x * x, -1, keepdims=True) + RMS_EPS) * g

def _gmlp_spatial_gate(u, v, v_g, v_b, w_s, b_s):
    bsz, seq, _ = v.shape
    pos = jnp.arange(GM_BLOCK)
    mask = (pos[:, None] // CHUNK) >= (pos[None, :] // CHUNK)
    w = jnp.where(mask[None], w_s, jnp.zeros_like(w_s))
    vn = _layer_norm(v, v_g, v_b).reshape(bsz, seq // GM_BLOCK, GM_BLOCK, GM_GROUPS, GM_GROUP_DIM)
    mixed = jnp.einsum("gts,bnsgc->bntgc", w, vn) + b_s.T[:, :, None]
    return u * mixed.reshape(bsz, seq, GM_WIDTH)

def _hgrn2(q_raw, f_raw, i_raw, g_raw, lb, o_g):
    bsz, seq, _ = q_raw.shape
    nc = seq // HG_CHUNK
    f32 = jnp.float32

    def heads(t, d):
        return t.astype(f32).reshape(bsz, nc, HG_CHUNK, HG_HEADS, d)

    lbf = lb.astype(f32)
    fr = f_raw.astype(f32)
    log_f = heads(jnp.log(lbf + (1.0 - lbf) * jax.nn.sigmoid(fr)), HG_DK)
    k = heads((1.0 - lbf) * jax.nn.sigmoid(-fr), HG_DK)
    q = heads(jax.nn.silu(q_raw.astype(f32)), HG_DK)
    v = heads(i_raw, HG_DV)
    b = jnp.cumsum(log_f, axis=2)
    q_dec = q * jnp.exp(b)
    k_dec = k * jnp.exp(-b)
    causal = jnp.tril(jnp.ones((HG_CHUNK, HG_CHUNK), f32))
    scores = jnp.einsum("bnthd,bnshd->bnhts", q_dec, k_dec) * causal
    o_intra = jnp.einsum("bnhts,bnshe->bnthe", scores, v)
    b_last = b[:, :, -1:]
    k_end = k * jnp.exp(b_last - b)
    decay = jnp.exp(b_last[:, :, 0])

    def step(state, xs):
        qc, kc, vc, dc = xs
        o = jnp.einsum("bthd,bhde->bthe", qc, state)
        state = dc[..., None] * state + jnp.einsum("bthd,bthe->bhde", kc, vc)
        return state, o

    s0 = jnp.zeros((bsz, HG_HEADS, HG_DK, HG_DV), f32)
    _, o_inter = lax.scan(step, s0, (jnp.moveaxis(q_dec, 1, 0), jnp.moveaxis(k_end, 1, 0),
                                     jnp.moveaxis(v, 1, 0), jnp.moveaxis(decay, 1, 0)))
    o = (o_intra + jnp.moveaxis(o_inter, 0, 1)).reshape(bsz, seq, HG_HEADS, HG_DV)
    o = _rms_norm(o, o_g.astype(f32).reshape(HG_HEADS, HG_DV)).reshape(bsz, seq, HG_WIDTH)
    o = o * jax.nn.silu(g_raw.astype(f32))
    return o.astype(q_raw.dtype)

def second_inputs(seed: int = 0) -> dict:
    key = jax.random.key(seed)
    ks = jax.random.split(key, 26)
    f32 = jnp.float32
    L = DEPTH_2

    def nrm(k, shape, scale):
        return jax.random.normal(k, shape, f32) * scale

    def gain(k, shape):
        return 1.0 + nrm(k, shape, 0.02)

    return {
        "x": nrm(ks[0], (BATCH, SEQ, D_MODEL), 1.0),
        "p": nrm(ks[1], (DEPTH_2, BATCH, SEQ, PLE_DIM), 1.0),
        "ln0_g": gain(ks[2], (D_MODEL,)),
        "ln0_b": nrm(ks[3], (D_MODEL,), 0.02),
        "w_in": nrm(ks[4], (L, D_MODEL, D_IN), D_MODEL ** -0.5),
        "b_in": nrm(ks[5], (L, D_IN), 0.02),
        "gm_norm_g": gain(ks[6], (L, GM_WIDTH)),
        "gm_norm_b": nrm(ks[7], (L, GM_WIDTH), 0.02),
        "gm_w_s": nrm(ks[8], (L, GM_GROUPS, GM_BLOCK, GM_BLOCK), 0.5 * GM_BLOCK ** -0.5),
        "gm_b_s": gain(ks[9], (L, GM_GROUPS, GM_BLOCK)),
        "hg_lb_logits": nrm(ks[10], (L + 1, HG_KWIDTH), 0.5),
        "hg_norm_g": gain(ks[11], (L, HG_WIDTH)),
        "w_a": nrm(ks[12], (L, GM_WIDTH, D_MODEL), BETA * GM_WIDTH ** -0.5),
        "w_b": nrm(ks[13], (L, HG_WIDTH, D_MODEL), BETA * HG_WIDTH ** -0.5),
        "w_o": nrm(ks[14], (L, D_MODEL, D_MODEL), BETA * D_MODEL ** -0.5),
        "ln1_g": gain(ks[15], (L, D_MODEL)),
        "ln1_b": nrm(ks[16], (L, D_MODEL), 0.02),
        "w_ffn_gate": nrm(ks[17], (L, D_MODEL, D_FF), D_MODEL ** -0.5),
        "w_ffn_up": nrm(ks[18], (L, D_MODEL, D_FF), BETA * D_MODEL ** -0.5),
        "w_ffn_down": nrm(ks[19], (L, D_FF, D_MODEL), BETA * D_FF ** -0.5),
        "w_ple": nrm(ks[20], (L, PLE_DIM, D_MODEL), PLE_DIM ** -0.5),
        "w_ple_gate": nrm(ks[21], (L, D_MODEL, D_MODEL), D_MODEL ** -0.5),
        "b_ple_gate": nrm(ks[22], (L, D_MODEL), 0.02),
        "ln2_g": gain(ks[23], (L, D_MODEL)),
        "ln2_b": nrm(ks[24], (L, D_MODEL), 0.02),
    }

def second_block(x, p, ln0_g, ln0_b, w_in, b_in, gm_norm_g, gm_norm_b, gm_w_s, gm_b_s,
              hg_lb_logits, hg_norm_g, w_a, w_b, w_o, ln1_g, ln1_b,
              w_ffn_gate, w_ffn_up, w_ffn_down, w_ple, w_ple_gate, b_ple_gate, ln2_g, ln2_b):
    lb_all = jnp.cumsum(jax.nn.softmax(hg_lb_logits.astype(jnp.float32), axis=0), axis=0)
    h = _layer_norm(x, ln0_g, ln0_b)
    for i in range(DEPTH_2):
        proj = jnp.einsum("bsd,de->bse", h, w_in[i]) + b_in[i]
        u_r, v_r, q_r, f_r, i_r, g_r, ga_r, gb_r = jnp.split(proj, IN_OFFSETS, axis=-1)
        y_a = _gmlp_spatial_gate(jax.nn.gelu(u_r), jax.nn.gelu(v_r), gm_norm_g[i], gm_norm_b[i],
                                 gm_w_s[i], gm_b_s[i])
        y_b = _hgrn2(q_r, f_r, i_r, g_r, lb_all[i], hg_norm_g[i])
        merged = (jax.nn.sigmoid(ga_r) * jnp.einsum("bsc,cd->bsd", y_a, w_a[i])
                  + jax.nn.sigmoid(gb_r) * jnp.einsum("bsc,cd->bsd", y_b, w_b[i]))
        mix = jnp.einsum("bsd,de->bse", merged, w_o[i])
        h1 = _layer_norm(ALPHA * h + mix, ln1_g[i], ln1_b[i])
        hid = jax.nn.silu(jnp.einsum("bsd,df->bsf", h1, w_ffn_gate[i])) * jnp.einsum("bsd,df->bsf", h1, w_ffn_up[i])
        ffn = jnp.einsum("bsf,fd->bsd", hid, w_ffn_down[i])
        ple = (jax.nn.sigmoid(jnp.einsum("bsd,de->bse", h1, w_ple_gate[i]) + b_ple_gate[i])
               * jnp.einsum("bsr,rd->bsd", p[i], w_ple[i]))
        h = _layer_norm(ALPHA * h1 + ffn + ple, ln2_g[i], ln2_b[i])
    return h


_first_inputs = second_inputs


def second_inputs(seed=0):
    import zlib

    import numpy as np

    out = dict(_first_inputs(seed))
    spreads = {}
    factors = {'ln0_g': 2.943,
     'ln0_b': 3.089,
     'b_in': 8.0,
     'gm_norm_g': 64.0,
     'gm_norm_b': 64.0,
     'gm_b_s': 36.12,
     'hg_lb_logits': 8.0,
     'hg_norm_g': 36.131,
     'ln1_g': 3.045,
     'ln1_b': 3.023,
     'b_ple_gate': 64.0,
     'ln2_g': 8.438,
     'ln2_b': 8.269}
    for name, (base, spread) in spreads.items():
        noise = np.random.default_rng([zlib.crc32(name.encode()), seed]).standard_normal(out[name].shape)
        drawn = base * np.exp(spread * noise) if base else spread * noise
        out[name] = __import__('jax').numpy.asarray(drawn.astype(out[name].dtype))
    for name, factor in factors.items():
        out[name] = (out[name] * factor).astype(out[name].dtype)
    return out


_narrow_inputs = second_inputs


def second_inputs(seed=0):

    out = dict(_narrow_inputs(seed))
    wider = {'gm_norm_g': 5.77,
     'gm_norm_b': 6.02,
     'gm_b_s': 4.66,
     'hg_norm_g': 4.64,
     'ln2_g': 3.27,
     'ln2_b': 3.27}
    for name, times in wider.items():
        mean = out[name].mean()
        out[name] = (mean + times * (out[name] - mean)).astype(out[name].dtype)
    return out


def setup_inputs(seed=0):
    out = dict(first_inputs(seed))
    for name, value in second_inputs(seed + 1).items():
        if name != "x":
            out[name + "_2"] = value
    return out


def reference(
    x, norm_g, w_in, b_gate, conv_dw, conv_b, conv_ln_g, conv_ln_b, ret_decay, q_norm_g,
    k_norm_g, attn_sink, w_conv_out, w_ret_out, w_attn_out, w_out, p_2, ln0_g_2, ln0_b_2,
    w_in_2, b_in_2, gm_norm_g_2, gm_norm_b_2, gm_w_s_2, gm_b_s_2, hg_lb_logits_2, hg_norm_g_2,
    w_a_2, w_b_2, w_o_2, ln1_g_2, ln1_b_2, w_ffn_gate_2, w_ffn_up_2, w_ffn_down_2, w_ple_2,
    w_ple_gate_2, b_ple_gate_2, ln2_g_2, ln2_b_2,
):
    x = first_block(
        x, norm_g, w_in, b_gate, conv_dw, conv_b, conv_ln_g, conv_ln_b, ret_decay, q_norm_g,
        k_norm_g, attn_sink, w_conv_out, w_ret_out, w_attn_out, w_out,
    )
    return second_block(
        x, p_2, ln0_g_2, ln0_b_2, w_in_2, b_in_2, gm_norm_g_2, gm_norm_b_2, gm_w_s_2, gm_b_s_2,
        hg_lb_logits_2, hg_norm_g_2, w_a_2, w_b_2, w_o_2, ln1_g_2, ln1_b_2, w_ffn_gate_2,
        w_ffn_up_2, w_ffn_down_2, w_ple_2, w_ple_gate_2, b_ple_gate_2, ln2_g_2, ln2_b_2,
    )


_drawn_inputs = setup_inputs


def setup_inputs(seed=0):
    import zlib

    import numpy as np

    out = dict(_drawn_inputs(seed))
    spreads = {}
    factors = {'conv_b': 3.066,
     'conv_ln_g': 5.144,
     'conv_ln_b': 5.909,
     'q_norm_g': 8.0,
     'k_norm_g': 8.0,
     'attn_sink': 8.0}
    for name, (base, spread) in spreads.items():
        noise = np.random.default_rng([zlib.crc32(name.encode()), seed]).standard_normal(out[name].shape)
        drawn = base * np.exp(spread * noise) if base else spread * noise
        out[name] = __import__('jax').numpy.asarray(drawn.astype(out[name].dtype))
    for name, factor in factors.items():
        out[name] = (out[name] * factor).astype(out[name].dtype)
    return out
```

```python
import concourse.bass as bass
from concourse import mybir
from contextlib import ExitStack

P = 128
T = 512
PRIMED = 1
D = 1024
NT = D // P
DEPTH = 2
TAPS = 31
PAD = TAPS // 2
CUTS = (14, 18, 22, 26, TAPS)
VW = T + 2 * PAD
HEADS = 4
CHUNK16 = 16
SEGMENTS = (16, 32, 64, 128)
FF = 2816
FF_GROUPS = (8, 8, 6)
ALPHA = 2.0 ** 0.25
RMS_EPS = 1e-6
LN_EPS = 1e-5

LAYER_GROUPS = 39
LAYER_USES = 43
GLU, QKV0, RET, RET3, ATT, ATT_OUT, CONV_GATE, CONV_OUT, RET_GATE, W_OUT = (
    (0, 0), (4, 4), (6, 6), (18, 21), (21, 25), (25, 29), (29, 33), (31, 35), (35, 39), (37, 41))
BLOCK_G = DEPTH * LAYER_GROUPS
BLOCK_U = DEPTH * LAYER_USES
HG, GM_V, HG_OUT, GM_U, GM_OUT, MIX_OUT, PLE = (0, 8, 10, 14, 16, 20, 22)
N_SLABS = 4 * BLOCK_G + 4 * 22 + 2 + 8 + 2 * 22 + 8 * 3

C_NORM, C_CB, C_CG, C_CLB = 0, 8, 16, 24
C_DW = 32
C_BG = C_DW + 8 * TAPS
C_QG, C_KG = C_BG + 24, C_BG + 25
C_SINK = C_BG + 26
C_RD = C_SINK + 16
NVEC = C_RD + 8
B_LN0, B_IN, B_GM, B_LB, B_OG, B_LN1, B_LN2, B_PLE = 0, 16, 80, 96, 112, 120, 136, 152
NVEC2 = 160

U_SIZE = 14208
U_A, U_B, U_C, U_VT, U_SG, U_T, U_VF, U_DT = 0, 2048, 4096, 6144, 8192, 10240, 12288, 13312


def build(nc, ins, out, xsave):
    f32, f32r, i16, i32 = mybir.dt.float32, mybir.dt.float32r, mybir.dt.int16, mybir.dt.int32
    A = mybir.ActivationFunctionType
    O = mybir.AluOpType
    AX = mybir.AxisListType.X
    ctx = ExitStack()
    with ctx:
        def sb(name, shape, dt=f32):
            return ctx.enter_context(nc.sbuf_tensor(name, shape, dt))

        raw = sb("raw", [P, 2, NT * P])
        whi = sb("whi", [P, 4, NT * P], f32r)
        wlo = sb("wlo", [P, 4, NT * P], f32r)
        hhi = sb("hhi", [P, NT, T], f32r)
        hlo = sb("hlo", [P, NT, T], f32r)
        zhi = sb("zhi", [P, NT, T], f32r)
        zlo = sb("zlo", [P, NT, T], f32r)
        cv = sb("cv", [P, NT, VW])
        yr = sb("yr", [P, NT, T])
        tab = sb("tab", [P, 2, T])
        amask = sb("amask", [P, 3 * P])
        ident = sb("ident", [P, P])
        ones = sb("ones", [P, P])
        blk64 = sb("blk64", [P, P])
        rot = sb("rot", [P, P])
        vec = sb("vec", [P, NVEC])
        vec2 = sb("vec2", [P, NVEC2])
        dist = sb("dist", [P, 896], i16)
        sm = sb("sm", [P, 112])
        lbs = sb("lbs", [P, 40])
        U = sb("U", [P, U_SIZE])
        gem = ctx.enter_context(nc.psum_tensor("gem", [P, 4, T], f32))
        xp = ctx.enter_context(nc.psum_tensor("xp", [P, 4, T], f32))

        def tiles(off, n, w=T):
            return U[:, off:off + n * w].rearrange("p (a b) -> p a b", a=n)

        def sbank(b):
            return (xp[:, 0, :], xp[:, 1, :], gem[:, 0, :])[b % 3]

        def tbank(b):
            return (xp[:, 2, :], gem[:, 1, :])[b % 2]

        QK, OT, ST, SG, TT, VF = (tiles(U_A, 4), tiles(U_B, 4), tiles(U_C, 4), tiles(U_SG, 4),
                                  tiles(U_T, 4), tiles(U_VF, 2))
        VT = tiles(U_VT, 4)
        DT = U[:, U_DT:U_DT + 896]
        RS = U[:, U_DT:U_DT + T]
        KA, KP = tiles(U_A, 2), U[:, U_A + 1024:U_A + 1536]
        VTA = tiles(U_VT, 4, 256)
        VP = tiles(U_VT + 1024, 4, P)
        QR = tiles(U_B, 4)
        PB = tiles(U_C, 3, 384)
        PT = tiles(U_C + 1152, 2, 384)
        ZT = tiles(U_VF, 2)
        MG, XN = tiles(U_A, 8), tiles(U_C, 8)
        F1, F2, BC, EB, ENB, E3, QS, KD = (U[:, n * T:(n + 1) * T] for n in range(8))
        KE, QD, VFH, SMK = (U[:, n * T:(n + 1) * T] for n in (8, 9, 10, 13))
        KT, VTK = tiles(11 * T, 4, P), tiles(12 * T, 4, P)
        KES, QDS = (dict(zip(SEGMENTS, [first] + [U[:, n * T:(n + 1) * T] for n in rest]))
                    for first, rest in ((KE, (14, 16, 18)), (QD, (15, 17, 19))))
        SS = tiles(20 * T, 3, P)
        at, DEC, KF, QF = 21 * T, {}, {}, {}
        for w in SEGMENTS:
            DEC[w], KF[w], QF[w] = (U[:, a:a + T // w] for a in range(at, at + 3 * T // w, T // w))
            at += 3 * T // w
        OH, OSQ, HT = (U[:, n * T:(n + 1) * T] for n in (22, 23, 24))
        VG = XC = tiles(0, 8)
        MG2 = PL = tiles(U_C, 8)
        SGB = tiles(U_SG, 4)
        GW = U[:, U_SG + 1024:U_SG + 2048].rearrange("p (a b) -> p a b", a=NT)
        GB = U[:, U_T + 1024:U_T + 2048].rearrange("p (a b) -> p a b", a=NT)
        VNT = tiles(U_VF, 2)
        GW2 = tiles(U_SG + 1024, 2)
        NEGLG, SK, NSK, DW = sm[:, 0:8], sm[:, 8:16], sm[:, 16:24], sm[:, 24:56]
        EPS, EPS5, ONE = sm[:, 56:57], sm[:, 57:58], sm[:, 58:59]
        MX, NM, RSUM, ES, DEN, REC = (sm[:, c:c + 3] for c in (59, 62, 65, 68, 71, 74))
        LB, OML, NBF, LBT = lbs[:, 0:8], lbs[:, 8:16], lbs[:, 16:24], lbs[:, 24:40]

        def sem(name):
            return ctx.enter_context(nc.semaphore(name))

        raw_in = [sem(f"raw_in{i}") for i in range(2)]
        hi_done, lo_done, slab_done = sem("hi_done"), sem("lo_done"), sem("slab_done")
        evac = [sem(f"evac{b}") for b in range(4)]
        const_in, x_in, x_out, tab_in, vec_in = (sem(n) for n in ("const_in", "x_in", "x_out", "tab_in", "vec_in"))
        gm_in, gb_in, p_in, out_done = (sem(n) for n in ("gm_in", "gb_in", "p_in", "out_done"))
        consts, passed = sem("consts"), sem("passed")
        sq_ready, sq_used, rstd = sem("sq_ready"), sem("sq_used"), sem("rstd")
        ln_mean, ln_cent, pre_ready = sem("ln_mean"), sem("ln_cent"), sem("pre_ready")
        h_ready, z_ready = sem("h_ready"), sem("z_ready")
        layer_done, out_ready = sem("layer_done"), sem("out_ready")
        lg_ready, dt_arg, dt_ready, roped = sem("lg_ready"), sem("dt_arg"), sem("dt_ready"), sem("roped")
        vt_done, vt_ready, score_done, st_ready = (sem(n) for n in ("vt_done", "vt_ready", "score_done", "st_ready"))
        pv_done, o_ready = sem("pv_done"), sem("o_ready")
        osum, omean, ocent, osq, ossq, ovar, orstd = (sem(n) for n in (
            "osum", "omean", "ocent", "osq", "ossq", "ovar", "orstd"))
        a_sq, a_ssq, a_rs, a_kn, a_rot, a_rope = (sem(n) for n in (
            "a_sq", "a_ssq", "a_rs", "a_kn", "a_rot", "a_rope"))
        kv_copied, s_done, m_ready, p_exp, p_ready = (sem(n) for n in (
            "kv_copied", "s_done", "m_ready", "p_exp", "p_ready"))
        t_done, t_ready, ao_done, ao_read = (sem(n) for n in ("t_done", "t_ready", "ao_done", "ao_read"))
        csum, cmean, cssq, cvar, crstd, cn, cs = (sem(n) for n in (
            "csum", "cmean", "cssq", "cvar", "crstd", "cn", "cs"))
        lb_arg, lb_exp, lb_ready = (sem(n) for n in ("lb_arg", "lb_exp", "lb_ready"))
        f_ready, lf_ready, scan_done, gap_ready, eb_ready, gap_exp, ke_ready, qd_ready = (sem(n) for n in (
            "f_ready", "lf_ready", "scan_done", "gap_ready", "eb_ready", "gap_exp", "ke_ready", "qd_ready"))
        klev_ready, lev_ready = sem("klev_ready"), sem("lev_ready")
        hg_t, hg_tr, hg_sc, hg_sel, hg_p, hg_up, hg_inter = (sem(n) for n in (
            "hg_t", "hg_tr", "hg_sc", "hg_sel", "hg_p", "hg_up", "hg_inter"))
        hg_osq, hg_var, hg_rstd = sem("hg_osq"), sem("hg_var"), sem("hg_rstd")
        vn_ready, vn_t, vnt_ready, gm_done, gm_read = (sem(n) for n in (
            "vn_ready", "vn_t", "vnt_ready", "gm_done", "gm_read"))
        sg_used = sem("sg_used")

        block = ctx.enter_context(nc.Block())

        def apart(eng):
            eng.sem_inc(passed, 1)

        @block.sync
        def _(sp):
            W = ins["slabs"]
            for s in range(2):
                sp.dma_start(raw[:, s, :], W[s]).then_inc(raw_in[s], 16)
            with sp.Fori(1, N_SLABS // 2) as g:
                for s in range(2):
                    sp.wait_ge(lo_done, g * 2 + (s - 1))
                    sp.dma_start(raw[:, s, :], W[g * 2 + s]).then_inc(raw_in[s], 16)

            for i in range(NT):
                sp.wait_ge(out_ready, i + 1)
                sp.dma_start(out[i], yr[:, i, :]).then_inc(out_done, 16)
            sp.wait_ge(out_done, 16 * NT)
            sp.wait_ge(x_out, 16 * (DEPTH + 1))

        @block.gpsimd
        def _(pool):
            pool.memset(ones[:, :], 1.0).then_inc(consts, 1)
            pool.memset(EPS, RMS_EPS).then_inc(consts, 1)
            pool.memset(EPS5, LN_EPS).then_inc(consts, 1)
            pool.memset(ONE, 1.0).then_inc(consts, 1)
            pool.memset(cv[:, :, 0:PAD], 0.0).then_inc(consts, 1)
            pool.memset(cv[:, :, PAD + T:VW], 0.0).then_inc(consts, 1)

            def low(G, k):
                pool.wait_ge(hi_done, G * 4 + (k + 1))
                pool.tensor_tensor(wlo[:, k % 4, :], raw[:, k % 2, :], whi[:, k % 4, :].bitcast(f32),
                                   O.subtract).then_inc(lo_done, 1)

            with pool.Fori(0, N_SLABS // 4) as G:
                for k in range(4):
                    low(G, k)
            for k in range(N_SLABS % 4):
                low(N_SLABS // 4, k)

        @block.tensor
        def _(pe):
            pe.sem_inc(slab_done, 1)
            pe.sem_inc(sq_used, 1)
            pe.wait_ge(consts, 1)
            pe.wait_ge(const_in, 16 * 6)

            def gemm(G, k, outs, first=None):
                pe.wait_ge(lo_done, G * 4 + (k + 1))
                for bank, uses, terms in outs:
                    pe.wait_ge(evac[bank], uses + PRIMED)
                    for n, (r, hi, lo) in enumerate(terms):
                        if first is not None:
                            pe.wait_ge(first[0], first[1] + (n + 1))
                        wh = whi[:, k % 4, r * P:(r + 1) * P]
                        wl = wlo[:, k % 4, r * P:(r + 1) * P]
                        o = gem[:, bank, :]
                        pe.matmul(o, wh, hi, start=(n == 0), stop=False)
                        pe.matmul(o, wh, lo, start=False, stop=False)
                        mm = pe.matmul(o, wl, hi, start=False, stop=(n == len(terms) - 1))
                mm.then_inc(slab_done, 1)

            def full(G, k, uses, hi, lo, n=NT, first=None, k0=0):
                gemm(G, k, [(k % 4, uses + (k - k0) // 4, [(r, hi[:, r, :], lo[:, r, :]) for r in range(n)])], first)

            def hslab(G, k, uses, first=None, k0=0):
                full(G, k, uses, hhi, hlo, first=first, k0=k0)

            def zslab(G, k, uses, first=None, n=NT, k0=0):
                full(G, k, uses, zhi, zlo, n, first, k0)

            def abreast(G, ks, uses, first, k0=0):
                for k in ks:
                    pe.wait_ge(lo_done, G * 4 + (k + 1))
                    pe.wait_ge(evac[k % 4], uses + (k - k0) // 4 + PRIMED)
                for r in range(NT):
                    pe.wait_ge(h_ready, first + (r + 1))
                    for k in ks:
                        wh, wl = (w[:, k % 4, r * P:(r + 1) * P] for w in (whi, wlo))
                        o = gem[:, k % 4, :]
                        pe.matmul(o, wh, hhi[:, r, :], start=(r == 0), stop=False)
                        pe.matmul(o, wh, hlo[:, r, :], start=False, stop=False)
                        mm = pe.matmul(o, wl, hhi[:, r, :], start=False, stop=(r == NT - 1))
                        if r == NT - 1:
                            mm.then_inc(slab_done, 1)

            def half(G, k, uses, first=None):
                gemm(G, k, [((2 * k + j) % 4, uses + (2 * k + j) // 4,
                             [(4 * j + r, zhi[:, r, :], zlo[:, r, :]) for r in range(4)]) for j in range(2)], first)

            def layer(L):
                g0, u0 = L * LAYER_GROUPS, L * LAYER_USES
                for i in range(NT):
                    pe.wait_ge(sq_ready, L * 8 + (i + 1))
                    pe.matmul(xp[:, 0, :], ones[:, :], TT[:, i % 2, :], start=(i == 0),
                              stop=(i == NT - 1)).then_inc(sq_used, 1)
                abreast(g0 + GLU[0], range(3), u0 + GLU[1], L * 8)
                hslab(g0 + GLU[0], 3, u0 + GLU[1])
                with pe.Fori(1, 4) as it:
                    for k in range(4):
                        hslab(g0 + (it + GLU[0]), k, u0 + (it + GLU[1]))

                def qkv(G, u, hd):
                    for k in range(4):
                        hslab(G, k, u)
                    for k in range(4, 8):
                        hslab(G, k, u)
                        if k > 4:
                            pe.wait_ge(evac[(k - 1) % 4], u + 2 + PRIMED)
                            turn(hd, k - 5)
                    pe.wait_ge(evac[3], u + 2 + PRIMED)
                    turn(hd, 3)

                def turn(hd, v):
                    pe.wait_ge(vt_ready, L * 18 + hd * 4 + max(v - 1, 0) + PRIMED)
                    for tb in range(4):
                        mm = pe.transpose(xp[:, 2 + v % 2, tb * P:(tb + 1) * P],
                                          VF[:, v % 2, tb * P:(tb + 1) * P], ident[:, :])
                    mm.then_inc(vt_done, 1)

                def scores(hd, j):
                    n = L * 16 + hd * 4
                    if j == 0:
                        pe.wait_ge(roped, L * 8 + hd * 2 + 2)
                        pe.wait_ge(vt_ready, L * 18 + hd * 4 + 4 + PRIMED)
                    if j >= 2:
                        pe.wait_ge(st_ready, n + (j - 1))
                    for r in range(2):
                        mm = pe.matmul(xp[:, 2 + j % 2, :], QK[:, 2 + r, j * P:(j + 1) * P], QK[:, r, :],
                                       start=(r == 0), stop=(r == 1))
                    mm.then_inc(score_done, 1)

                def pv(hd, v):
                    if v == 0:
                        pe.wait_ge(st_ready, L * 16 + hd * 4 + 4)
                    for j in range(4):
                        mm = pe.matmul(xp[:, v, :], VT[:, j, v * P:(v + 1) * P], ST[:, j, :],
                                       start=(j == 0), stop=(j == 3))
                    mm.then_inc(pv_done, 1)

                def gates(G, u, hd):
                    hslab(G, 0, u)
                    scores(hd, 0)
                    scores(hd, 1)
                    hslab(G, 1, u)
                    scores(hd, 2)
                    scores(hd, 3)
                    hslab(G, 2, u)
                    pv(hd, 0)
                    pv(hd, 1)
                    hslab(G, 3, u)
                    pv(hd, 2)
                    pv(hd, 3)

                def mean(hd):
                    pe.wait_ge(osum, L * 4 + hd + 1)
                    pe.matmul(xp[:, 0, :], ones[:, :], TT[:, 2, :], start=True, stop=True).then_inc(omean, 1)

                def var(hd):
                    pe.wait_ge(ossq, L * 4 + hd + 1)
                    pe.matmul(xp[:, 1, :], ones[:, :], TT[:, 2, :], start=True, stop=True).then_inc(ovar, 1)

                def ret_out(G, u, hd):
                    for k in range(4):
                        half(G, k, u, (z_ready, L * 40 + hd * 4 + PRIMED) if k == 0 else None)

                qkv(g0 + QKV0[0], u0 + QKV0[1], 0)
                with pe.Fori(0, 3) as hd:
                    G, u = g0 + (hd * 4 + RET[0]), u0 + (hd * 5 + RET[1])
                    gates(G, u, hd)
                    Gn, un = G + 1, u + 1
                    hslab(Gn, 0, un)
                    mean(hd)
                    hslab(Gn, 1, un)
                    hslab(Gn, 2, un)
                    hslab(Gn, 3, un)
                    var(hd)
                    for k in range(4, 8):
                        hslab(Gn, k, un)
                        if k > 4:
                            pe.wait_ge(evac[(k - 1) % 4], un + 2 + PRIMED)
                            turn(hd + 1, k - 5)
                    pe.wait_ge(evac[3], un + 2 + PRIMED)
                    turn(hd + 1, 3)
                    ret_out(G + 3, u + 3, hd)
                G, u = g0 + RET3[0], u0 + RET3[1]
                gates(G, u, 3)
                hslab(G + 1, 0, u + 1)
                mean(3)
                hslab(G + 1, 1, u + 1)
                hslab(G + 1, 2, u + 1)
                var(3)
                hslab(G + 1, 3, u + 1)
                for v in range(2):
                    pe.wait_ge(evac[2 + v], u + 2 + PRIMED)
                    for tb in range(4):
                        mm = pe.transpose(xp[:, 2 + v, tb * P:(tb + 1) * P],
                                          VF[:, v, tb * P:(tb + 1) * P], ident[:, :])
                    mm.then_inc(vt_done, 1)
                ret_out(G + 2, u + 2, 3)

                def a_norm(n):
                    pe.wait_ge(a_sq, L * 10 + n + 1)
                    pe.matmul(xp[:, 0, :], blk64[:, :], TT[:, 0, :], start=True, stop=True).then_inc(a_ssq, 1)

                def a_turn(n, src):
                    pe.wait_ge(a_kn, L * 10 + n + 1)
                    pe.matmul(xp[:, 1, :], rot[:, :], src, start=True, stop=True).then_inc(a_rot, 1)

                with pe.Fori(0, 2) as pr:
                    G, u = g0 + (pr * 2 + ATT[0]), u0 + (pr * 2 + ATT[1])
                    qn, bn = pr * 5 + 1, L * 64 + pr * 32
                    hslab(G, 0, u)
                    a_norm(pr * 5)
                    hslab(G, 1, u)
                    a_turn(pr * 5, KP)
                    a_norm(qn)
                    for m in range(3):
                        hslab(G, m + 2, u)
                        a_turn(qn + m, QR[:, m, :])
                        a_norm(qn + (m + 1))
                    hslab(G, 5, u)
                    a_turn(qn + 3, QR[:, 3, :])

                    def qk(b):
                        m, hf, n = b // 8, b // 4 % 2, b % 4
                        if b == 2:
                            pe.wait_ge(evac[0], u + 2 + PRIMED)
                        if b == 0:
                            pe.wait_ge(kv_copied, L * 2 + pr + 1)
                            pe.wait_ge(a_rope, L * 10 + qn + 4)
                        if b >= 3:
                            pe.wait_ge(p_exp, bn + (b - 2))
                        lo, hi = max(n - 1, 0), min(n + 2, 4)
                        c = (lo - n + 1) * P
                        pe.matmul(sbank(b)[:, c:c + (hi - lo) * P], QR[hf * 64:hf * 64 + 64, m, n * P:(n + 1) * P],
                                  KP[hf * 64:hf * 64 + 64, lo * P:hi * P], start=True, stop=True)\
                            .then_inc(s_done, 1)

                    def turn_p(b):
                        n = b % 4
                        pe.wait_ge(p_ready, bn + (b + 1))
                        if b == 1:
                            pe.wait_ge(evac[1], u + 2 + PRIMED)
                        if b >= 2:
                            pe.wait_ge(t_ready, bn + (b - 1))
                        for j in range(max(n - 1, 0), min(n + 2, 4)):
                            c = j - n + 1
                            mm = pe.transpose(tbank(b)[:, c * P:(c + 1) * P], PB[:, b % 3, c * P:(c + 1) * P], ident[:, :])
                        mm.then_inc(t_done, 1)

                    def a_pv(b):
                        hf, n = b // 4 % 2, b % 4
                        pe.wait_ge(t_ready, bn + (b + 1))
                        if n == 0 and b:
                            pe.wait_ge(ao_read, (L * 16 + pr * 8) + b // 4)
                        lo, hi = max(n - 1, 0), min(n + 2, 4)
                        for j in range(lo, hi):
                            c = j - n + 1
                            mm = pe.matmul(xp[hf * 64:hf * 64 + 64, 3, n * P:(n + 1) * P],
                                           VP[:, j, hf * 64:hf * 64 + 64], PT[:, b % 2, c * P:(c + 1) * P],
                                           start=(j == lo), stop=(j == hi - 1))
                        if n == 3:
                            mm.then_inc(ao_done, 1)

                    qk(0)
                    qk(1)
                    for b in range(32):
                        if b + 2 < 32:
                            qk(b + 2)
                        if b % 16 == 0:
                            hslab(G, 6 + b // 16, u)
                        if b >= 2:
                            a_pv(b - 2)
                        turn_p(b)
                    a_pv(30)
                    a_pv(31)

                def branch_out(G, u, first=None):
                    hslab(G, 0, u)
                    zslab(G, 1, u, first)
                    hslab(G, 2, u)
                    zslab(G, 3, u)

                G, u = g0 + ATT_OUT[0], u0 + ATT_OUT[1]
                branch_out(G, u, (z_ready, L * 40 + 16 + PRIMED))
                branch_out(G + 1, u + 1)
                pe.wait_ge(csum, L + 1)
                pe.matmul(xp[:, 0, :], ones[:, :], TT[:, 0, :], start=True, stop=True).then_inc(cmean, 1)
                with pe.Fori(2, 4) as it:
                    branch_out(G + it, u + it)
                pe.wait_ge(cssq, L + 1)
                pe.matmul(xp[:, 1, :], ones[:, :], TT[:, 0, :], start=True, stop=True).then_inc(cvar, 1)
                with pe.Fori(0, 2) as it:
                    for k in range(4):
                        hslab(g0 + (it + CONV_GATE[0]), k, u0 + (it + CONV_GATE[1]))
                with pe.Fori(0, 4) as it:
                    branch_out(g0 + (it + CONV_OUT[0]), u0 + (it + CONV_OUT[1]), (z_ready, L * 40 + 24 + PRIMED))
                with pe.Fori(0, 2) as it:
                    for k in range(4):
                        hslab(g0 + (it + RET_GATE[0]), k, u0 + (it + RET_GATE[1]))
                with pe.Fori(0, 2) as it:
                    for k in range(4):
                        zslab(g0 + (it + W_OUT[0]), k, u0 + (it + W_OUT[1]), (z_ready, L * 40 + 32 + PRIMED) if k == 0 else None)

            with pe.Fori(0, DEPTH) as L:
                layer(L)

            def ln_stats(n, src, ready):
                for i in range(NT):
                    ready(i)
                    mm = pe.matmul(xp[:, 0, :], ones[:, :], src(i), start=(i == 0), stop=(i == NT - 1))
                mm.then_inc(ln_mean, 1)

            def ln_squares(n):
                for i in range(NT):
                    pe.wait_ge(sq_ready, 8 * (DEPTH + n) + i + 1)
                    pe.matmul(xp[:, 1, :], ones[:, :], TT[:, i % 2, :], start=(i == 0),
                              stop=(i == NT - 1)).then_inc(sq_used, 1)

            pe.wait_ge(layer_done, DEPTH + PRIMED)
            ln_stats(0, lambda i: XN[:, i, :], lambda i: None)
            ln_squares(0)
            G, u = BLOCK_G + HG, BLOCK_U + HG
            abreast(G, range(3), u, 8 * DEPTH)
            hslab(G, 3, u)

            def head_products(p, G, u):
                def rows(a, b):
                    for n in range(a, b):
                        k, r = n // NT, n % NT
                        if r == 0:
                            pe.wait_ge(lo_done, G * 4 + (k + 1))
                            pe.wait_ge(evac[k], u + PRIMED)
                        wh, wl = (w[:, k, r * P:(r + 1) * P] for w in (whi, wlo))
                        pe.matmul(gem[:, k, :], wh, hhi[:, r, :], start=(r == 0), stop=False)
                        pe.matmul(gem[:, k, :], wh, hlo[:, r, :], start=False, stop=False)
                        mm = pe.matmul(gem[:, k, :], wl, hhi[:, r, :], start=False, stop=(r == NT - 1))
                        if r == NT - 1:
                            mm.then_inc(slab_done, 1)

                def score(bank, keys, queries):
                    for tb in range(4):
                        c = slice(tb * P, (tb + 1) * P)
                        mm = pe.matmul(xp[:, bank, c], keys[:, c], queries[:, c], start=True, stop=True)
                    mm.then_inc(hg_sc, 1)

                pe.wait_ge(klev_ready, p + 1)
                pe.wait_ge(evac[1], BLOCK_U + 1 + p + PRIMED)
                for n, src in enumerate((KES[P], VFH)):
                    for tb in range(4):
                        mm = pe.transpose(xp[:, n, tb * P:(tb + 1) * P], src[:, tb * P:(tb + 1) * P], ident[:, :])
                    mm.then_inc(hg_t, 1)
                rows(0, 3)
                pe.wait_ge(lev_ready, p + 1)
                pe.wait_ge(hg_rstd, p + PRIMED)
                score(3, KES[16], QDS[16])
                score(2, KD, QDS[16])
                rows(3, 8)
                pe.wait_ge(hg_tr, p * 2 + 1)
                score(0, KES[32], QDS[32])
                pe.wait_ge(hg_tr, p * 2 + 2)
                score(1, KES[64], QDS[64])
                rows(8, 14)
                pe.wait_ge(hg_sel, p * 4 + 4)
                for tb in range(3):
                    mm = pe.matmul(xp[:, 2, tb * P:(tb + 1) * P], KT[:, tb, :], VTK[:, tb, :], start=True, stop=True)
                mm.then_inc(hg_p, 1)
                for tb in range(4):
                    c = slice(tb * P, (tb + 1) * P)
                    pe.matmul(xp[:, 3, c], VTK[:, tb, :], SMK[:, c], start=(tb == 0), stop=False, skip_group_check=True)
                rows(14, 18)
                pe.wait_ge(hg_up, p + 1)
                for tb in range(1, 4):
                    c = slice(tb * P, (tb + 1) * P)
                    mm = pe.matmul(xp[:, 3, c], SS[:, tb - 1, :], QDS[P][:, c], start=False, stop=(tb == 3),
                                   skip_group_check=True)
                mm.then_inc(hg_inter, 1)
                rows(18, 22)
                pe.wait_ge(hg_osq, p + 1)
                pe.matmul(xp[:, 2, :], ones[:, :], OSQ, start=True, stop=True).then_inc(hg_var, 1)
                rows(22, 32)

            with pe.Fori(0, 7) as p:
                head_products(p, BLOCK_G + 1 + p, BLOCK_U + 1 + p)
            Gv, uv = BLOCK_G + GM_V, BLOCK_U + GM_V
            head_products(7, Gv, uv)
            for k in range(4, 8):
                hslab(Gv, k, uv)
            Go, uo = BLOCK_G + HG_OUT, BLOCK_U + HG_OUT

            def branch_out(G, u, first=None):
                hslab(G, 0, u)
                zslab(G, 1, u, first)
                hslab(G, 2, u)
                zslab(G, 3, u)

            Z0 = DEPTH * 40
            branch_out(Go, uo, (z_ready, Z0 + PRIMED))
            ln_stats(1, lambda i: VG[:, i, :], lambda i: None)
            branch_out(Go + 1, uo + 1)
            ln_squares(1)
            with pe.Fori(2, 4) as it:
                branch_out(Go + it, uo + it)

            def spatial(i):
                pe.wait_ge(vnt_ready, i + 1)
                if i >= 2:
                    pe.wait_ge(gm_read, i - 1)
                for tb in range(4):
                    mm = pe.matmul(xp[:, 2 + i % 2, tb * P:(tb + 1) * P], VNT[:, i % 2, tb * P:(tb + 1) * P],
                                   GW[:, i, :], start=True, stop=True)
                mm.then_inc(gm_done, 1)

            for i in range(NT):
                hslab(BLOCK_G + GM_U, i, BLOCK_U + GM_U)
                pe.wait_ge(vn_ready, i + 1)
                for tb in range(4):
                    mm = pe.transpose(xp[:, i % 2, tb * P:(tb + 1) * P], VG[:, i, tb * P:(tb + 1) * P], ident[:, :])
                mm.then_inc(vn_t, 1)
                if i:
                    spatial(i - 1)
            spatial(7)
            with pe.Fori(0, 4) as it:
                branch_out(BLOCK_G + (it + GM_OUT), BLOCK_U + (it + GM_OUT), (z_ready, Z0 + 8 + PRIMED))
            with pe.Fori(0, 2) as it:
                for k in range(4):
                    zslab(BLOCK_G + (it + MIX_OUT), k, BLOCK_U + (it + MIX_OUT),
                          (z_ready, Z0 + 16 + PRIMED) if k == 0 else None)
            Gp, up = BLOCK_G + PLE, BLOCK_U + PLE
            for k in range(2):
                gemm(Gp, k, [(j, up + k, [(2 * j + r, hhi[:, 6 + r, :], hlo[:, 6 + r, :]) for r in range(2)])
                             for j in range(4)], (h_ready, 8 * DEPTH + 8))
            ln_stats(2, lambda i: XC[:, i, :], lambda i: pe.wait_ge(pre_ready, i + 1))
            ln_squares(2)
            abreast(Gp, range(2, 5), up + 2, 8 * DEPTH + 10, k0=2)
            for k in range(5, 10):
                hslab(Gp, k, up + 2, k0=2)
            m0, z0 = 0, Z0 + 24
            for n in FF_GROUPS:
                with pe.Fori(0, n // 2) as it:
                    for k in range(2, 6):
                        hslab(Gp + (it + (2 + m0 // 4)), k, up + (it + (4 + m0 // 4)), k0=2)
                m0 += 2 * n
                with pe.Fori(0, 2) as it:
                    for k in range(2, 6):
                        zslab(Gp + (it + (2 + m0 // 4)), k, up + (it + (4 + m0 // 4)),
                              (z_ready, z0 + PRIMED) if k == 2 else None, n, k0=2)
                m0, z0 = m0 + 8, z0 + n
            ln_stats(3, lambda i: cv[:, i, 0:T], lambda i: pe.wait_ge(pre_ready, 8 + i + 1))
            ln_squares(3)

        @block.scalar
        def _(act):
            for b in range(4):
                act.sem_inc(evac[b], 1)
            act.sem_inc(vt_ready, 1)
            act.sem_inc(hg_rstd, 1)
            act.dma_start(XN, ins["x"]).then_inc(x_in, 16)
            for n, (dst, name) in enumerate(((ident, "ident"), (blk64, "blk64"), (rot, "rot"), (amask, "amask"),
                                             (dist, "dist"), (vec2, "vec2"))):
                act.dma_start(dst[:, :], ins[name]).then_inc(const_in, 16)

            def high(G, k, free=True):
                act.wait_ge(raw_in[k % 2], G * 32 + 16 * (k // 2 + 1))
                if free:
                    act.wait_ge(slab_done, G * 4 + (k - 3) + PRIMED)
                act.activation(whi[:, k % 4, :], raw[:, k % 2, :], A.Copy).then_inc(hi_done, 1)

            def tick(G, k):
                high(G, k + 3)
                act.wait_ge(slab_done, G * 4 + (k + 1) + PRIMED)

            def read(k, dst, func, bias=0.0, scale=1.0, bank=None):
                b = k % 4 if bank is None else bank
                act.activation(dst, gem[:, b, :], func, bias=bias, scale=scale).then_inc(evac[b], 1)

            def inv_sqrt(dst, src, n, eps, count):
                act.activation(dst, src, A.Ln, bias=eps, scale=1.0 / n)
                act.drain()
                act.activation(dst, dst, A.Exp, scale=-0.5).then_inc(count, 1)

            for k in range(3):
                high(0, k, False)
            act.dma_start(xsave[0], ins["x"]).then_inc(x_out, 16)

            def layer(L):
                g0, u0 = L * LAYER_GROUPS, L * LAYER_USES
                act.wait_ge(layer_done, L + PRIMED)
                act.dma_start(vec[:, :], ins["vecs"][L]).then_inc(vec_in, 16)
                act.dma_start(tab[:, :, :], ins["tab_ret"]).then_inc(tab_in, 16)
                act.wait_ge(x_in, L * 16 + 16)
                act.wait_ge(consts, 6)
                for i in range(NT):
                    if i >= 2:
                        act.wait_ge(sq_used, L * 8 + (i - 1) + PRIMED)
                    act.activation(TT[:, i % 2, :], XN[:, i, :], A.Square).then_inc(sq_ready, 1)
                act.wait_ge(sq_used, L * 8 + 8 + PRIMED)
                inv_sqrt(RS, xp[:, 0, :], D, EPS, rstd)
                with act.Fori(0, 4) as it:
                    for k in range(4):
                        tick(g0 + (it + GLU[0]), k)
                        if k % 2 == 0:
                            act.wait_ge(evac[k + 1], u0 + (it + GLU[1]) + PRIMED)
                            read(k, SG[:, k // 2, :], A.Sigmoid)
                act.wait_ge(vec_in, L * 16 + 16)
                act.activation(NEGLG, vec[:, C_RD:C_RD + 8], A.Exp).then_inc(lg_ready, 1)
                act.wait_ge(x_out, L * 16 + 16)

                def turned(hd, v):
                    n = L * 18 + hd * 4 + (v + 1)
                    act.wait_ge(vt_done, n)
                    act.activation(VT[:, :, v * P:(v + 1) * P],
                                   xp[:, 2 + v % 2, :].rearrange("p (a b) -> p a b", a=4), A.Copy)\
                        .then_inc(vt_ready, 1)

                def qk_tick(G, k):
                    tick(G, k)
                    read(k, QK[:, k, :], A.Copy, scale=(1.0 if k < 2 else 1.0 / 16))

                def v_ticks(G, hd):
                    for v in range(4):
                        tick(G, 4 + v)
                        read(4 + v, VF[:, v % 2, :], A.Copy)
                        if v:
                            turned(hd, v - 1)
                    turned(hd, 3)

                def o_read(hd, v):
                    act.wait_ge(pv_done, L * 16 + hd * 4 + (v + 1))
                    act.activation(OT[:, v, :], xp[:, v, :], A.Copy).then_inc(o_ready, 1)

                def gates(G, hd):
                    act.wait_ge(dt_arg, L * 4 + hd + 1)
                    act.activation(DT, DT, A.Exp).then_inc(dt_ready, 1)
                    for k in range(4):
                        tick(G, k)
                        act.wait_ge(z_ready, L * 40 + hd * 4 + PRIMED)
                        read(k, SG[:, k, :], A.Silu)
                        if k == 3:
                            o_read(hd, 0)
                            o_read(hd, 1)
                    o_read(hd, 2)
                    o_read(hd, 3)

                def squares(hd):
                    for v in range(4):
                        act.wait_ge(ocent, L * 16 + hd * 4 + (v + 1))
                        act.activation(ST[:, v, :], OT[:, v, :], A.Square).then_inc(osq, 1)

                G = g0 + QKV0[0]
                for k in range(4):
                    qk_tick(G, k)
                v_ticks(G, 0)
                with act.Fori(0, 3) as hd:
                    G = g0 + (hd * 4 + RET[0])
                    gates(G, hd)
                    for k in range(3):
                        qk_tick(G + 1, k)
                    squares(hd)
                    qk_tick(G + 1, 3)
                    act.wait_ge(ovar, L * 4 + hd + 1)
                    inv_sqrt(RS, xp[:, 1, :], T, EPS, orstd)
                    v_ticks(G + 1, hd + 1)
                    for k in range(4):
                        high(G + 3, k + 3)
                G = g0 + RET3[0]
                gates(G, 3)
                act.wait_ge(roped, L * 8 + 8)
                act.dma_start(tab[:, :, :], ins["tab_att"]).then_inc(tab_in, 16)
                for k in range(2):
                    tick(G + 1, k)
                    read(k, KA[:, k, :], A.Copy)
                squares(3)
                tick(G + 1, 2)
                read(2, VF[:, 0, :], A.Copy)
                act.wait_ge(ovar, L * 4 + 4)
                inv_sqrt(RS, xp[:, 1, :], T, EPS, orstd)
                tick(G + 1, 3)
                read(3, VF[:, 1, :], A.Copy)
                for v in range(2):
                    act.wait_ge(vt_done, L * 18 + 16 + v + 1)
                    act.activation(VTA[:, :, v * P:(v + 1) * P],
                                   xp[:, 2 + v, :].rearrange("p (a b) -> p a b", a=4), A.Copy)\
                        .then_inc(vt_ready, 1)
                for k in range(4):
                    high(G + 2, k + 3)

                def a_inv(n):
                    act.wait_ge(a_ssq, L * 10 + n + 1)
                    inv_sqrt(RS, xp[:, 0, :], 64, EPS, a_rs)

                act.wait_ge(z_ready, L * 40 + 16 + PRIMED)
                with act.Fori(0, 2) as pr:
                    G, u = g0 + (pr * 2 + ATT[0]), u0 + (pr * 2 + ATT[1])
                    bn = L * 64 + pr * 32
                    for k in range(4):
                        tick(G, k)
                        read(k, QR[:, k, :], A.Copy)
                        a_inv(pr * 5 + k)
                    for m in range(2):
                        tick(G, 4 + m)
                        read(m, SG[:, m, :], A.Silu)
                        if m == 0:
                            a_inv(pr * 5 + 4)

                    def exps(b):
                        n = b % 4
                        lo, hi = max(1 - n, 0) * P, min(5 - n, 3) * P
                        act.wait_ge(m_ready, bn + (b + 1))
                        if b >= 3:
                            act.wait_ge(t_done, bn + (b - 2))
                        r = b % 3
                        act.activation(PB[:, r, lo:hi], sbank(b)[:, lo:hi], A.Exp, bias=NM[:, r:r + 1], scale=0.125,
                                       accum_out=RSUM[:, r:r + 1])
                        act.activation(ES[:, r:r + 1], NM[:, r:r + 1], A.Exp,
                                       bias=SK[:, (b // 8 + b // 4 % 2 * 4):(b // 8 + b // 4 % 2 * 4) + 1])\
                            .then_inc(p_exp, 1)

                    def turned_p(b):
                        n = b % 4
                        lo, hi = max(1 - n, 0) * P, min(5 - n, 3) * P
                        act.wait_ge(t_done, bn + (b + 1))
                        act.activation(PT[:, b % 2, lo:hi], tbank(b)[:, lo:hi], A.Copy).then_inc(t_ready, 1)

                    exps(0)
                    exps(1)
                    for b in range(32):
                        if b % 16 == 0:
                            tick(G, 6 + b // 16)
                            read(2 + b // 16, SG[:, 2 + b // 16, :], A.Silu)
                        turned_p(b)
                        if b + 2 < 32:
                            exps(b + 2)

                act.wait_ge(z_ready, L * 40 + 24 + PRIMED)
                act.dma_start(XN, xsave[L]).then_inc(x_in, 16)

                def gate_ticks(ph, base):
                    with act.Fori(0, 4) as it:
                        G, u = g0 + (it + ph[0]), u0 + (it + ph[1])
                        for k in range(4):
                            tick(G, k)
                            if k % 2 == 0:
                                act.wait_ge(evac[k + 1], u + PRIMED)
                                read(k, SG[:, k // 2, :], A.Sigmoid, bias=vec[:, bass.ds(it * 2 + (base + k // 2), 1)])

                def merged(use):
                    act.wait_ge(evac[1], u0 + use + PRIMED)
                    act.wait_ge(evac[3], u0 + use + PRIMED)

                gate_ticks(ATT_OUT, C_BG + 16)
                act.wait_ge(cvar, L + 1)
                inv_sqrt(RS, xp[:, 1, :], D, EPS, crstd)
                merged(CONV_GATE[1])
                with act.Fori(0, 2) as it:
                    for k in range(4):
                        tick(g0 + (it + CONV_GATE[0]), k)
                        i = it * 4 + k
                        act.wait_ge(z_ready, L * 40 + 24 + it * 4 + PRIMED)
                        read(k, SG[:, k, :], A.Silu)
                        act.wait_ge(cn, L * 8 + i + 1)
                        act.activation(TT[:, 2 + k % 2, :], TT[:, k % 2, :], A.Silu,
                                       bias=vec[:, bass.ds(i + C_CLB, 1)], scale=vec[:, bass.ds(i + C_CG, 1)])\
                            .then_inc(cs, 1)
                act.wait_ge(z_ready, L * 40 + 32 + PRIMED)
                gate_ticks(CONV_OUT, C_BG)
                merged(RET_GATE[1])
                with act.Fori(0, 2) as it:
                    for k in range(4):
                        tick(g0 + (it + RET_GATE[0]), k)
                        act.wait_ge(z_ready, L * 40 + 32 + it * 4 + PRIMED)
                        read(k, SG[:, k, :], A.Sigmoid, bias=vec[:, bass.ds(it * 4 + (C_BG + 8 + k), 1)])
                with act.Fori(0, 2) as it:
                    for k in range(4):
                        high(g0 + (it + W_OUT[0]), k + 3)
                act.wait_ge(layer_done, L + 1 + PRIMED)
                act.dma_start(xsave[L + 1], XN).then_inc(x_out, 16)

            with act.Fori(0, DEPTH) as L:
                layer(L)

            act.dma_start(tab[:, :, :], ins["tab_hg"]).then_inc(tab_in, 16)

            def col(c, i):
                return vec2[:, c + i:c + i + 1] if isinstance(i, int) else vec2[:, bass.ds(i + c, 1)]

            def ln_squares(n, src):
                for i in range(NT):
                    act.wait_ge(ln_cent, 8 * n + i + 1)
                    act.wait_ge(sq_used, 8 * (DEPTH + n) + (i - 1) + PRIMED)
                    act.activation(TT[:, i % 2, :], src(i), A.Square).then_inc(sq_ready, 1)
                act.wait_ge(sq_used, 8 * (DEPTH + n) + 8 + PRIMED)
                inv_sqrt(RS, xp[:, 1, :], D, EPS5, rstd)

            ln_squares(0, lambda i: XN[:, i, :])
            act.wait_ge(lb_arg, 1)
            act.activation(LBT, LBT, A.Exp).then_inc(lb_exp, 1)
            f_n = B_IN + 24

            def el_f(G, hd):
                tick(G, 0)
                act.wait_ge(ke_ready, hd * 2 + PRIMED)
                act.activation(F1, gem[:, 0, :], A.Sigmoid, bias=col(f_n, hd))
                nbf = NBF[:, hd:hd + 1] if isinstance(hd, int) else NBF[:, bass.ds(hd, 1)]
                read(0, F2, A.Sigmoid, bias=nbf, scale=-1.0)
                act.wait_ge(f_ready, hd + 1)
                act.activation(BC, F1, A.Ln).then_inc(lf_ready, 1)

            def el_i(G, hd):
                tick(G, 1)
                read(1, VFH, A.Identity, bias=col(B_IN + 32, hd))

            def el_exp(hd):
                act.wait_ge(scan_done, hd + 1)
                act.activation(EB, BC, A.Exp)
                act.activation(ENB, BC, A.Exp, scale=-1.0).then_inc(eb_ready, 1)
                act.wait_ge(gap_ready, hd + 1)
                act.activation(E3, F1, A.Exp).then_inc(gap_exp, 1)

            def el_q(G, hd):
                tick(G, 2)
                act.wait_ge(qd_ready, hd + PRIMED)
                read(2, QS, A.Silu, bias=col(B_IN + 16, hd))

            def el_g(G, hd):
                tick(G, 3)
                dst = cv[:, hd, 0:T]
                read(3, dst, A.Silu, bias=col(B_IN + 40, hd))

            act.wait_ge(lb_ready, 1)
            G = BLOCK_G + HG
            el_f(G, 0)
            el_i(G, 0)
            el_exp(0)
            el_q(G, 0)
            el_g(G, 0)

            def head_turned(p):
                for n, dst in enumerate((KT, VTK)):
                    act.wait_ge(hg_t, p * 2 + (n + 1))
                    act.activation(dst, xp[:, n, :].rearrange("p (a b) -> p a b", a=4), A.Copy)\
                        .then_inc(hg_tr, 1)

            def head_norm(p):
                act.wait_ge(hg_inter, p + 1)
                act.wait_ge(z_ready, DEPTH * 40 + p + PRIMED)
                act.activation(OH, xp[:, 3, :], A.Copy)
                act.drain()
                act.activation(OSQ, OH, A.Square).then_inc(hg_osq, 1)
                act.wait_ge(hg_var, p + 1)
                inv_sqrt(RS, xp[:, 2, :], P, EPS, hg_rstd)

            with act.Fori(0, 7) as p:
                G, hd = BLOCK_G + 1 + p, p + 1
                head_turned(p)
                el_f(G, hd)
                el_i(G, hd)
                el_exp(hd)
                head_norm(p)
                el_q(G, hd)
                el_g(G, hd)
            head_turned(7)
            G = BLOCK_G + GM_V
            for k in range(8):
                tick(G, k)
                if k == 0:
                    act.wait_ge(hg_sc, 32)
                    act.wait_ge(lev_ready, 8)
                read(k, VG[:, k, :], A.Gelu_apprx_tanh, bias=col(B_IN + 8, k))
                if k == 1:
                    head_norm(7)
            act.wait_ge(z_ready, DEPTH * 40 + 8 + PRIMED)

            def gates2(G, u, base):
                for k in range(4):
                    tick(G, k)
                    if k % 2 == 0:
                        act.wait_ge(evac[k + 1], u + PRIMED)
                        read(k, SGB[:, k // 2, :], A.Sigmoid, bias=base(k // 2))

            G, u = BLOCK_G + HG_OUT, BLOCK_U + HG_OUT
            hb = B_IN + 56
            gates2(G, u, lambda r: col(hb, r))
            act.dma_start(GW, ins["gm_w"]).then_inc(gm_in, 16)
            gates2(G + 1, u + 1, lambda r: col(hb, 2 + r))
            ln_squares(1, lambda i: VG[:, i, :])
            act.dma_start(GB, ins["gm_b"]).then_inc(gb_in, 16)
            with act.Fori(2, 4) as it:
                gates2(G + it, u + it, lambda r: col(hb, it * 2 + r))

            for i in range(NT):
                tick(BLOCK_G + GM_U, i)
                read(i, cv[:, i, 0:T], A.Gelu_apprx_tanh, bias=col(B_IN, i))
                act.wait_ge(vn_t, i + 1)
                act.activation(VNT[:, i % 2, :], xp[:, i % 2, :], A.Copy).then_inc(vnt_ready, 1)
            u = BLOCK_U + GM_OUT
            act.wait_ge(evac[1], u + PRIMED)
            act.wait_ge(evac[3], u + PRIMED)
            with act.Fori(0, 4) as it:
                gates2(BLOCK_G + (it + GM_OUT), BLOCK_U + (it + GM_OUT), lambda r: col(B_IN + 48, it * 2 + r))
            act.wait_ge(z_ready, DEPTH * 40 + 16 + PRIMED)
            act.dma_start(GW2, ins["p"]).then_inc(p_in, 16)
            with act.Fori(0, 2) as it:
                for k in range(4):
                    high(BLOCK_G + (it + MIX_OUT), k + 3)
            Gp, up = BLOCK_G + PLE, BLOCK_U + PLE
            act.wait_ge(z_ready, DEPTH * 40 + 24 + PRIMED)
            for k in range(2):
                tick(Gp, k)
                for j in range(4):
                    read(j, PL[:, k * 4 + j, :], A.Copy)
            ln_squares(2, lambda i: XC[:, i, :])
            for k in range(2, 10):
                tick(Gp, k)
                act.wait_ge(sg_used, max(k - 2 - 3, 0) + PRIMED)
                read(k, SGB[:, k % 4, :], A.Sigmoid, bias=col(B_PLE, k - 2))
            m0 = 0
            for g, n in enumerate(FF_GROUPS):
                with act.Fori(0, n // 2) as it:
                    for k in range(2, 6):
                        Gf = Gp + (it + (2 + m0 // 4))
                        tick(Gf, k)
                        if k % 2 == 0:
                            act.wait_ge(z_ready, it * 2 + (DEPTH * 40 + 24 + sum(FF_GROUPS[:g])) + PRIMED)
                            act.wait_ge(sg_used, 8 + PRIMED)
                            read(k, SGB[:, (k - 2) // 2, :], A.Silu)
                m0 += 2 * n
                if g < 2:
                    with act.Fori(0, 2) as it:
                        for k in range(2, 6):
                            high(Gp + (it + (2 + m0 // 4)), k + 3)
                else:
                    for k in range(2, 7):
                        high(Gp + (2 + m0 // 4), k + 3)
                m0 += 8
            ln_squares(3, lambda i: cv[:, i, 0:T])

        @block.vector
        def _(dve):
            tt, ts, stt = dve.tensor_tensor, dve.tensor_scalar, dve.scalar_tensor_tensor
            dve.sem_inc(z_ready, 1)
            dve.sem_inc(ke_ready, 1)
            dve.sem_inc(qd_ready, 1)
            dve.sem_inc(sg_used, 1)
            dve.sem_inc(layer_done, 1)
            dve.wait_ge(const_in, 16 * 6)
            dve.wait_ge(consts, 6)

            def split(hi, lo, src, count):
                dve.tensor_copy(hi, src)
                dve.drain()
                tt(lo, src, hi.bitcast(f32), O.subtract).then_inc(count, 1)

            def layer(L):
                g0, u0 = L * LAYER_GROUPS, L * LAYER_USES

                def product(G, k):
                    dve.wait_ge(slab_done, G * 4 + (k + 1) + PRIMED)

                dve.wait_ge(vec_in, L * 16 + 16)
                dve.wait_ge(x_in, L * 16 + 16)
                dve.wait_ge(rstd, L + 1)
                for i in range(NT):
                    stt(TT[:, i % 2, :], XN[:, i, :], vec[:, C_NORM + i:C_NORM + i + 1], RS, O.mult, O.mult)
                    dve.drain()
                    split(hhi[:, i, :], hlo[:, i, :], TT[:, i % 2, :], h_ready)
                with dve.Fori(0, 4) as it:
                    G, u = g0 + (it + GLU[0]), u0 + (it + GLU[1])
                    for k in (1, 3):
                        product(G, k)
                        dve.wait_ge(evac[k - 1], u + 1 + PRIMED)
                        tt(cv[:, it * 2 + k // 2, PAD:PAD + T], gem[:, k, :], SG[:, k // 2, :], O.mult)\
                            .then_inc(evac[k], 1)
                dve.memset(yr[:, :, :], 0.0)

                def conv(i, first=0, end=TAPS):
                    if first == 0:
                        dve.drain()
                        dve.tensor_copy(DW[:, 0:TAPS], vec[:, bass.ds(i * TAPS + C_DW, TAPS)])
                        dve.tensor_copy(DW[:, TAPS:TAPS + 1], vec[:, bass.ds(i + C_CB, 1)])
                        dve.drain()
                    for n in range(first, end):
                        a, v = TT[:, n % 2, :], cv[:, i, n:n + T]
                        if n < 2:
                            ts(a, v, DW[:, n:n + 1], None, O.mult)
                        else:
                            stt(a, v, DW[:, n:n + 1], a, O.mult, O.add)
                        if n % 2:
                            dve.drain()
                    if end == TAPS:
                        dve.drain()
                        stt(cv[:, i, PAD:PAD + T], TT[:, 0, :], DW[:, TAPS:TAPS + 1], TT[:, 1, :], O.add, O.add)
                        dve.drain()

                def decay_arg(hd):
                    dve.drain()
                    fwd, bwd = ((NEGLG[:, c + hd:c + hd + 1] if isinstance(hd, int) else NEGLG[:, bass.ds(hd + c, 1)])
                                for c in (0, HEADS))
                    ts(U[:, U_T:U_T + 896], dist[:, :], fwd, -1.0, O.mult, O.mult)
                    dve.drain()
                    stt(DT, dist[:, :], bwd, U[:, U_T:U_T + 896], O.mult, O.min).then_inc(dt_arg, 1)

                def rope(G, u, r):
                    x1, x2 = QK[:, 2 * r, :], QK[:, 2 * r + 1, :]
                    cos, sin = tab[:, 0, :], tab[:, 1, :]
                    dve.wait_ge(evac[2 * r], u + 1 + PRIMED)
                    dve.wait_ge(evac[2 * r + 1], u + 1 + PRIMED)
                    tt(TT[:, 0, :], x1, cos, O.mult)
                    tt(TT[:, 1, :], x2, sin, O.mult)
                    tt(TT[:, 2, :], x2, cos, O.mult)
                    tt(TT[:, 3, :], x1, sin, O.mult)
                    dve.drain()
                    tt(x1, TT[:, 0, :], TT[:, 1, :], O.subtract)
                    tt(x2, TT[:, 2, :], TT[:, 3, :], O.add).then_inc(roped, 1)

                def mask_scores(hd):
                    dve.wait_ge(dt_ready, L * 4 + hd + 1)
                    for j in range(4):
                        dve.wait_ge(score_done, L * 16 + hd * 4 + (j + 1))
                        tt(ST[:, j, :], xp[:, 2 + j % 2, :], DT[:, 384 - j * P:896 - j * P], O.mult)\
                            .then_inc(st_ready, 1)

                def sum4(src, ready, n, count):
                    dve.drain()
                    dve.wait_ge(ready, n)
                    tt(TT[:, 2, :], src[:, 0, :], src[:, 1, :], O.add)
                    tt(TT[:, 3, :], src[:, 2, :], src[:, 3, :], O.add)
                    dve.drain()
                    tt(TT[:, 2, :], TT[:, 2, :], TT[:, 3, :], O.add).then_inc(count, 1)

                def center(hd):
                    dve.wait_ge(omean, L * 4 + hd + 1)
                    for v in range(4):
                        stt(OT[:, v, :], xp[:, 0, :], -1.0 / T, OT[:, v, :], O.mult, O.add).then_inc(ocent, 1)

                def gated(hd):
                    dve.drain()
                    dve.wait_ge(orstd, L * 4 + hd + 1)
                    for v in range(4):
                        tt(OT[:, v, :], OT[:, v, :], RS, O.mult)
                    dve.drain()
                    for v in range(4):
                        tt(OT[:, v, :], OT[:, v, :], SG[:, v, :], O.mult)
                    dve.drain()
                    for v in range(4):
                        split(zhi[:, v, :], zlo[:, v, :], OT[:, v, :], z_ready)

                def add_out(G, u, i=None):
                    for k in range(4):
                        product(G, k)
                        for j in range(2):
                            b, o = (2 * k + j) % 4, 2 * k + j
                            tt(yr[:, o, :], gem[:, b, :], yr[:, o, :], O.add).then_inc(evac[b], 1)
                        if i is not None:
                            conv(i, CUTS[k], CUTS[k + 1])

                G, u = g0 + QKV0[0], u0 + QKV0[1]
                dve.drain()
                dve.wait_ge(lg_ready, L + 1)
                dve.wait_ge(tab_in, L * 32 + 16)
                rope(G, u, 0)
                dve.drain()
                rope(G, u, 1)
                dve.drain()
                with dve.Fori(0, 3) as hd:
                    G, u = g0 + (hd * 4 + RET[0]), u0 + (hd * 5 + RET[1])
                    decay_arg(hd)
                    mask_scores(hd)
                    dve.drain()
                    conv(hd * 2)
                    sum4(OT, o_ready, L * 16 + hd * 4 + 4, osum)
                    center(hd)
                    dve.drain()
                    rope(G + 1, u + 1, 0)
                    dve.drain()
                    sum4(ST, osq, L * 16 + hd * 4 + 4, ossq)
                    dve.drain()
                    dve.wait_ge(ovar, L * 4 + hd + 1)
                    rope(G + 1, u + 1, 1)
                    dve.drain()
                    gated(hd)
                    conv(hd * 2 + 1, 0, CUTS[0])
                    add_out(G + 3, u + 3, hd * 2 + 1)
                    dve.drain()
                G, u = g0 + RET3[0], u0 + RET3[1]
                decay_arg(3)
                mask_scores(3)
                dve.drain()
                conv(6)
                sum4(OT, o_ready, L * 16 + 16, osum)
                center(3)
                dve.drain()
                sum4(ST, osq, L * 16 + 16, ossq)
                gated(3)
                add_out(G + 2, u + 2)

                def square(x, ready=None, n=0):
                    dve.drain()
                    if ready is not None:
                        dve.wait_ge(ready, n)
                    tt(TT[:, 0, :], x, x, O.mult).then_inc(a_sq, 1)

                def a_norm_rope(n, x, gcol, then):
                    dve.wait_ge(a_rs, L * 10 + n + 1)
                    stt(x, x, gcol, RS, O.mult, O.mult).then_inc(a_kn, 1)
                    then()
                    dve.drain()
                    tt(TT[:, 1, :], x, tab[:, 0, :], O.mult)
                    dve.wait_ge(a_rot, L * 10 + n + 1)
                    tt(TT[:, 2, :], xp[:, 1, :], tab[:, 1, :], O.mult)
                    dve.drain()
                    tt(x, TT[:, 1, :], TT[:, 2, :], O.add).then_inc(a_rope, 1)

                dve.drain()
                dve.wait_ge(tab_in, L * 32 + 32)
                dve.wait_ge(evac[0], u + 2 + PRIMED)
                dve.wait_ge(evac[1], u + 2 + PRIMED)
                dve.wait_ge(vt_ready, L * 18 + 18 + PRIMED)
                apart(dve)
                with dve.Fori(0, 2) as pr:
                    G, u = g0 + (pr * 2 + ATT[0]), u0 + (pr * 2 + ATT[1])
                    qn, bn = pr * 5 + 1, L * 64 + pr * 32
                    dve.tensor_copy(KP, KA[:, pr, :])
                    dve.tensor_copy(SK, vec[:, bass.ds(pr * 8 + C_SINK, 8)])
                    dve.tensor_copy(VP, VTA[:, :, bass.ds(pr * P, P)]).then_inc(kv_copied, 1)
                    dve.drain()
                    ts(NSK, SK, -1.0, None, O.mult)

                    def square_q(k):
                        square(QR[:, k, :], evac[k], u + 1 + PRIMED)

                    square(KP)
                    a_norm_rope(pr * 5, KP, vec[:, C_KG:C_KG + 1], lambda: square_q(0))
                    for k in range(4):
                        a_norm_rope(qn + k, QR[:, k, :], vec[:, C_QG:C_QG + 1],
                                    (lambda: square_q(k + 1)) if k < 3 else (lambda: None))
                    dve.drain()

                    def maxes(b):
                        n, r = b % 4, b % 3
                        lo, hi = max(1 - n, 0) * P, min(5 - n, 3) * P
                        c = b // 8 + b // 4 % 2 * 4
                        dve.wait_ge(s_done, bn + (b + 1))
                        apart(dve)
                        dve.tensor_tensor_reduce(sbank(b)[:, lo:hi], sbank(b)[:, lo:hi], amask[:, lo:hi], 1.0, -3e38,
                                                 O.add, O.max, MX[:, r:r + 1])
                        dve.drain()
                        ts(NM[:, r:r + 1], MX[:, r:r + 1], -0.125, NSK[:, c:c + 1], O.mult, O.min)\
                            .then_inc(m_ready, 1)

                    def normalise(b):
                        n, r = b % 4, b % 3
                        lo, hi = max(1 - n, 0) * P, min(5 - n, 3) * P
                        dve.wait_ge(p_exp, bn + (b + 1))
                        tt(DEN[:, r:r + 1], RSUM[:, r:r + 1], ES[:, r:r + 1], O.add)
                        dve.drain()
                        dve.reciprocal(REC[:, r:r + 1], DEN[:, r:r + 1])
                        dve.drain()
                        ts(PB[:, r, lo:hi], PB[:, r, lo:hi], REC[:, r:r + 1], None, O.mult).then_inc(p_ready, 1)

                    def head_out(q):
                        m, hf = q // 2, q % 2
                        dve.wait_ge(ao_done, L * 16 + pr * 8 + (q + 1))
                        if q % 2 == 0:
                            dve.wait_ge(evac[m], u + 2 + PRIMED)
                        rows = slice(hf * 64, hf * 64 + 64)
                        tt(ZT[rows, m % 2, :], xp[rows, 3, :], SG[rows, m, :], O.mult).then_inc(ao_read, 1)
                        if hf:
                            dve.drain()
                            split(zhi[:, pr * 4 + m, :], zlo[:, pr * 4 + m, :], ZT[:, m % 2, :], z_ready)

                    maxes(0)
                    maxes(1)
                    for b in range(32):
                        normalise(b)
                        if b + 2 < 32:
                            maxes(b + 2)
                        if b % 4 == 1 and b > 1:
                            head_out(b // 4 - 1)
                    head_out(7)
                    dve.drain()
                conv(7)
                y = [cv[:, i, PAD:PAD + T] for i in range(NT)]

                def sum8(get, acc):
                    tt(acc, get(0), get(1), O.add)
                    for i in range(2, NT):
                        dve.drain()
                        last = tt(acc, acc, get(i), O.add)
                    return last

                G, u = g0 + ATT_OUT[0], u0 + ATT_OUT[1]
                sum8(lambda i: y[i], TT[:, 0, :]).then_inc(csum, 1)

                def merge_first(it):
                    for k in (1, 3):
                        product(G + it, k)
                        dve.wait_ge(evac[k - 1], u + it + 1 + PRIMED)
                        tt(MG[:, it * 2 + k // 2, :], gem[:, k, :], SG[:, k // 2, :], O.mult)\
                            .then_inc(evac[k], 1)

                merge_first(0)
                merge_first(1)
                dve.wait_ge(cmean, L + 1)
                for i in range(NT):
                    stt(y[i], xp[:, 0, :], -1.0 / D, y[i], O.mult, O.add)
                dve.drain()
                tt(TT[:, 0, :], y[0], y[0], O.mult)
                for i in range(1, NT):
                    tt(TT[:, 1 + i % 2, :], y[i], y[i], O.mult)
                    dve.drain()
                    last = tt(TT[:, 0, :], TT[:, 0, :], TT[:, 1 + i % 2, :], O.add)
                last.then_inc(cssq, 1)
                with dve.Fori(2, 4) as it:
                    merge_first(it)
                dve.wait_ge(crstd, L + 1)
                apart(dve)
                with dve.Fori(0, 2) as it:
                    for k in range(4):
                        i = it * 4 + k
                        tt(TT[:, k % 2, :], cv[:, i, PAD:PAD + T], RS, O.mult).then_inc(cn, 1)
                        product(g0 + (it + CONV_GATE[0]), k)
                        dve.wait_ge(evac[k], u0 + (it + CONV_GATE[1] + 1) + PRIMED)
                        dve.wait_ge(cs, L * 8 + i + 1)
                        tt(TT[:, 2 + k % 2, :], TT[:, 2 + k % 2, :], SG[:, k, :], O.mult)
                        dve.drain()
                        split(zhi[:, i, :], zlo[:, i, :], TT[:, 2 + k % 2, :], z_ready)
                        dve.drain()
                with dve.Fori(0, 4) as it:
                    for k in (1, 3):
                        i = it * 2 + k // 2
                        product(g0 + (it + CONV_OUT[0]), k)
                        dve.wait_ge(evac[k - 1], u0 + (it + CONV_OUT[1] + 1) + PRIMED)
                        tt(TT[:, k // 2, :], gem[:, k, :], SG[:, k // 2, :], O.mult).then_inc(evac[k], 1)
                        dve.drain()
                        tt(MG[:, i, :], MG[:, i, :], TT[:, k // 2, :], O.add)
                        dve.drain()
                with dve.Fori(0, 2) as it:
                    for k in range(4):
                        i = it * 4 + k
                        dve.wait_ge(evac[k], u0 + (it + RET_GATE[1] + 1) + PRIMED)
                        tt(TT[:, k % 2, :], yr[:, i, :], SG[:, k, :], O.mult)
                        dve.drain()
                        tt(TT[:, k % 2, :], MG[:, i, :], TT[:, k % 2, :], O.add)
                        dve.drain()
                        split(zhi[:, i, :], zlo[:, i, :], TT[:, k % 2, :], z_ready)
                        dve.drain()
                dve.wait_ge(x_in, L * 16 + 32)
                apart(dve)
                with dve.Fori(0, 2) as it:
                    for k in range(4):
                        i = it * 4 + k
                        product(g0 + (it + W_OUT[0]), k)
                        tt(XN[:, i, :], gem[:, k, :], XN[:, i, :], O.add).then_inc(evac[k], 1)
                dve.drain().then_inc(layer_done, 1)

            with dve.Fori(0, DEPTH) as L:
                layer(L)

            def col(c, i):
                return vec2[:, c + i:c + i + 1] if isinstance(i, int) else vec2[:, bass.ds(i + c, 1)]

            def product(G, k):
                dve.wait_ge(slab_done, G * 4 + (k + 1) + PRIMED)

            def ln_center(n, src):
                dve.wait_ge(ln_mean, n + 1)
                for i in range(NT):
                    stt(src(i), xp[:, 0, :], -1.0 / D, src(i), O.mult, O.add).then_inc(ln_cent, 1)

            def ln_scale(n, src, dst, gcol, each):
                dve.wait_ge(rstd, DEPTH + n + 1)
                for i in range(NT):
                    tt(src(i), src(i), RS, O.mult)
                    dve.drain()
                    each(i, ts(dst(i), src(i), col(gcol, i), col(gcol + NT, i), O.mult, O.add))

            l0, l1 = vec2[:, B_LB:B_LB + 8], vec2[:, B_LB + 8:B_LB + 16]
            tt(LB, l0, l1, O.max)
            dve.drain()
            tt(LBT[:, 0:8], l0, LB, O.subtract)
            tt(LBT[:, 8:16], l1, LB, O.subtract).then_inc(lb_arg, 1)
            ts(NBF, vec2[:, B_IN + 24:B_IN + 32], -1.0, None, O.mult)
            dve.wait_ge(x_out, 16 * (DEPTH + 1))
            ln_center(0, lambda i: XN[:, i, :])

            def h_split(i, ins_):
                dve.drain()
                split(hhi[:, i, :], hlo[:, i, :], yr[:, i, :], h_ready)

            ln_scale(0, lambda i: XN[:, i, :], lambda i: yr[:, i, :], B_LN0, h_split)
            dve.wait_ge(lb_exp, 1)
            tt(OML, LBT[:, 0:8], LBT[:, 8:16], O.add)
            dve.drain()
            dve.reciprocal(OML, OML)
            dve.drain()
            tt(LB, LBT[:, 0:8], OML, O.mult)
            dve.drain()
            ts(OML, LB, -1.0, 1.0, O.mult, O.add).then_inc(lb_ready, 1)
            dve.wait_ge(tab_in, DEPTH * 32 + 16)
            dve.memset(U[:, 21 * T:22 * T], 1.0)
            dve.drain()
            BU = BLOCK_U + HG

            def lcol(t, i):
                return t[:, i:i + 1] if isinstance(i, int) else t[:, bass.ds(i, 1)]

            def el_f(hd):
                dve.wait_ge(evac[0], BU + 1 + hd + PRIMED)
                ts(F1, F1, lcol(OML, hd), lcol(LB, hd), O.mult, O.add).then_inc(f_ready, 1)

            def chunks(t):
                return t.rearrange("p (c s) -> p c s", s=CHUNK16)

            def el_scan(hd):
                dve.wait_ge(lf_ready, hd + 1)
                dve.tensor_tensor_scan(BC, tab[:, 0, :], BC, 0.0, O.mult, O.add).then_inc(scan_done, 1)
                dve.drain()
                last = chunks(BC)[:, :, CHUNK16 - 1:CHUNK16].to_broadcast([P, T // CHUNK16, CHUNK16])
                tt(chunks(F1), last, chunks(BC), O.subtract).then_inc(gap_ready, 1)

            def el_k(hd):
                dve.wait_ge(eb_ready, hd + 1)
                stt(KD, F2, lcol(OML, hd), ENB, O.mult, O.mult).then_inc(ke_ready, 1)
                dve.wait_ge(gap_exp, hd + 1)
                stt(KE, F2, lcol(OML, hd), E3, O.mult, O.mult).then_inc(ke_ready, 1)

            def half(t, n):
                return t.rearrange("p (s h) -> p s h", h=2)[:, :, n]

            def longer(dst, src, factor):
                n = factor.shape[-1]
                return tt(dst.rearrange("p (a b) -> p a b", a=n), src.rearrange("p (a b) -> p a b", a=n),
                          factor[:, :, None].to_broadcast([P, n, T // n]), O.mult)

            def k_levels():
                dve.tensor_copy(DEC[16], chunks(EB)[:, :, CHUNK16 - 1])
                dve.drain()
                for w in (16, 32, 64):
                    dve.tensor_copy(half(KF[w], 0), half(DEC[w], 1))
                    dve.tensor_copy(half(QF[w], 1), half(DEC[w], 0))
                    tt(DEC[2 * w], half(DEC[w], 0), half(DEC[w], 1), O.mult)
                    dve.drain()
                    last = longer(KES[2 * w], KES[w], KF[w])
                last.then_inc(klev_ready, 1)

            def el_q(hd):
                dve.wait_ge(evac[2], BU + 1 + hd + PRIMED)
                tt(QD, QS, EB, O.mult).then_inc(qd_ready, 1)
                for w in (16, 32, 64):
                    dve.drain()
                    last = longer(QDS[2 * w], QDS[w], QF[w])
                last.then_inc(lev_ready, 1)

            el_f(0)
            el_scan(0)
            el_k(0)
            k_levels()
            el_q(0)
            dve.drain()

            MASK = {w: tab[:, 1, n * P:(n + 1) * P] for n, w in enumerate((CHUNK16, 32, 64, 128))}

            def select(p):
                def blocks(t):
                    return t.rearrange("p (a b) -> p a b", a=4)

                dve.wait_ge(hg_sc, p * 4 + 1)
                tt(blocks(SMK), blocks(xp[:, 3, :]), MASK[32][:, None, :].to_broadcast([P, 4, P]),
                   O.mult).then_inc(hg_sel, 1)
                dve.drain()
                for n, (w, bank) in enumerate(((CHUNK16, 2), (64, 0), (128, 1))):
                    dve.wait_ge(hg_sc, p * 4 + (n + 2))
                    apart(dve)
                    dve.copy_predicated(blocks(SMK), MASK[w].bitcast(i32)[:, None, :].to_broadcast([P, 4, P]),
                                        blocks(xp[:, bank, :])).then_inc(hg_sel, 1)
                    dve.drain()

            def update(p):
                dve.wait_ge(hg_p, p + 1)
                dve.tensor_copy(SS[:, 0, :], xp[:, 2, 0:P])
                dve.drain()
                for tb in (1, 2):
                    last = stt(SS[:, tb, :], SS[:, tb - 1, :], DEC[P][:, tb:tb + 1], xp[:, 2, tb * P:(tb + 1) * P],
                               O.mult, O.add)
                    if tb == 1:
                        dve.drain()
                last.then_inc(hg_up, 1)

            def head_end(p):
                dve.wait_ge(hg_rstd, p + 1 + PRIMED)
                stt(OH, OH, col(B_OG, p), RS, O.mult, O.mult)
                dve.drain()
                tt(HT, OH, cv[:, p, 0:T], O.mult)
                dve.drain()
                split(zhi[:, p, :], zlo[:, p, :], HT, z_ready)

            with dve.Fori(0, 7) as p:
                hd = p + 1
                select(p)
                el_f(hd)
                update(p)
                el_scan(hd)
                el_k(hd)
                k_levels()
                head_end(p)
                el_q(hd)
                dve.drain()
            select(7)
            update(7)
            head_end(7)
            dve.drain()

            def merge(G, u, tile, first):
                for k in (1, 3):
                    product(G, k)
                    dve.wait_ge(evac[k - 1], u + 1 + PRIMED)
                    m = MG2[:, tile(k // 2), :]
                    if first:
                        tt(m, gem[:, k, :], SGB[:, k // 2, :], O.mult).then_inc(evac[k], 1)
                    else:
                        tt(TT[:, k // 2, :], gem[:, k, :], SGB[:, k // 2, :], O.mult).then_inc(evac[k], 1)
                        dve.drain()
                        tt(m, m, TT[:, k // 2, :], O.add)
                        dve.drain()

            G, u = BLOCK_G + HG_OUT, BLOCK_U + HG_OUT
            merge(G, u, lambda r: r, True)
            ln_center(1, lambda i: VG[:, i, :])
            merge(G + 1, u + 1, lambda r: 2 + r, True)
            with dve.Fori(2, 4) as it:
                merge(G + it, u + it, lambda r: it * 2 + r, True)
            dve.wait_ge(gm_in, 16)
            dve.memset(GW[64:P, :, 0:64], 0.0)
            ln_scale(1, lambda i: VG[:, i, :], lambda i: VG[:, i, :], B_GM, lambda i, x: x.then_inc(vn_ready, 1))
            dve.wait_ge(gb_in, 16)
            for i in range(NT):
                dve.wait_ge(gm_done, i + 1)
                tt(TT[:, 0, :].rearrange("p (a b) -> p a b", a=4), xp[:, 2 + i % 2, :].rearrange("p (a b) -> p a b", a=4),
                   GB[:, i:i + 1, :].to_broadcast([P, 4, P]), O.add).then_inc(gm_read, 1)
                dve.drain()
                dve.wait_ge(evac[i % 4], BLOCK_U + GM_U + i // 4 + 1 + PRIMED)
                tt(TT[:, 1, :], TT[:, 0, :], cv[:, i, 0:T], O.mult)
                dve.drain()
                split(zhi[:, i, :], zlo[:, i, :], TT[:, 1, :], z_ready)
                dve.drain()
            with dve.Fori(0, 4) as it:
                merge(BLOCK_G + (it + GM_OUT), BLOCK_U + (it + GM_OUT), lambda r: it * 2 + r, False)
            for i in range(NT):
                split(zhi[:, i, :], zlo[:, i, :], MG2[:, i, :], z_ready)
            dve.wait_ge(p_in, 16)
            for i in range(2):
                split(hhi[:, 6 + i, :], hlo[:, 6 + i, :], GW2[:, i, :], h_ready)
            with dve.Fori(0, 2) as it:
                for k in range(4):
                    i = it * 4 + k
                    product(BLOCK_G + (it + MIX_OUT), k)
                    stt(XC[:, i, :], yr[:, i, :], ALPHA, gem[:, k, :], O.mult, O.add).then_inc(evac[k], 1)
            dve.drain().then_inc(pre_ready, 8)
            ln_center(2, lambda i: XC[:, i, :])
            Gp, up = BLOCK_G + PLE, BLOCK_U + PLE
            product(Gp, 1)
            ln_scale(2, lambda i: XC[:, i, :], lambda i: yr[:, i, :], B_LN1, h_split)
            dve.drain()
            for k in range(2, 10):
                i = k - 2
                dve.wait_ge(evac[k % 4], up + 3 + (k - 2) // 4 + PRIMED)
                tt(TT[:, k % 2, :], SGB[:, k % 4, :], PL[:, i, :], O.mult).then_inc(sg_used, 1)
                dve.drain()
                stt(cv[:, i, 0:T], yr[:, i, :], ALPHA, TT[:, k % 2, :], O.mult, O.add)
                dve.drain()
            m0, z0 = 0, 0
            for n in FF_GROUPS:
                with dve.Fori(0, n // 2) as it:
                    G, u = Gp + (it + (2 + m0 // 4)), up + (it + (4 + m0 // 4))
                    for k in (3, 5):
                        product(G, k)
                        dve.wait_ge(evac[(k - 1) % 4], u + 1 + PRIMED)
                        j = (k - 3) // 2
                        tt(TT[:, j, :], gem[:, k % 4, :], SGB[:, j, :], O.mult).then_inc(evac[k % 4], 1)
                        dve.drain()
                        split(zhi[:, it * 2 + j, :], zlo[:, it * 2 + j, :], TT[:, j, :], z_ready)
                        dve.drain()
                m0 += 2 * n
                with dve.Fori(0, 2) as it:
                    for k in range(2, 6):
                        product(Gp + (it + (2 + m0 // 4)), k)
                        y = cv[:, it * 4 + (k - 2), 0:T]
                        tt(y, gem[:, k % 4, :], y, O.add).then_inc(evac[k % 4], 1)
                dve.drain()
                m0 += 8
            dve.drain().then_inc(pre_ready, 8)
            ln_center(3, lambda i: cv[:, i, 0:T])
            ln_scale(3, lambda i: cv[:, i, 0:T], lambda i: yr[:, i, :], B_LN2, lambda i, x: x.then_inc(out_ready, 1))


def _matmul_layout(m, cols=None):
    k, n = m.shape
    return m.reshape(k // P, P, n // P, P).transpose(2, 1, 0, 3)


def kernel(**inputs):
    import numpy as np
    import concourse.bacc as bacc
    from concourse.bass_utils import run_bass_kernel_spmd

    f = np.float32
    a = {k: np.asarray(v) for k, v in inputs.items()}

    slabs = []

    def put(tiles):
        slabs.append(tiles.reshape(tiles.shape[0], P, NT * P))

    heads = [8 * p + 4 * h + m for p in range(2) for m in range(4) for h in range(2)]
    perm = np.concatenate([np.arange(64 * h, 64 * h + 64) for h in heads])
    for l in range(DEPTH):
        w = _matmul_layout(a["w_in"][l])
        conv_a, conv_b, conv_gate, rq, rk, rv, rg = (w[o:o + n] for o, n in (
            (0, 8), (8, 8), (16, 8), (24, 8), (32, 8), (40, 16), (56, 16)))
        o = 72 * P
        aq = _matmul_layout(a["w_in"][l][:, o:o + D][:, perm])
        ak, av = w[80:82], w[82:84]
        ag = _matmul_layout(a["w_in"][l][:, 84 * P:92 * P][:, perm])
        gl = w[92:116]
        for i in range(NT):
            put(conv_b[i:i + 1])
            put(conv_a[i:i + 1])

        def qkv(h):
            put(rq[2 * h:2 * h + 2])
            put(rk[2 * h:2 * h + 2])
            put(rv[4 * h:4 * h + 4])

        wr = a["w_ret_out"][l].reshape(HEADS, 4, P, 4, 2, P)

        def ret_out(h):
            put(wr[h].transpose(2, 1, 3, 0, 4))

        qkv(0)
        for h in range(HEADS):
            put(rg[4 * h:4 * h + 4])
            if h < HEADS - 1:
                qkv(h + 1)
            else:
                put(ak)
                put(av)
            ret_out(h)
        for p in range(2):
            put(aq[4 * p:4 * p + 4])
            put(ag[4 * p:4 * p + 4])
        wa = _matmul_layout(a["w_attn_out"][l][perm])
        wc = _matmul_layout(a["w_conv_out"][l])
        for i in range(NT):
            put(gl[16 + i:17 + i])
            put(wa[i:i + 1])
        put(conv_gate)
        for i in range(NT):
            put(gl[i:i + 1])
            put(wc[i:i + 1])
        put(gl[8:16])
        put(_matmul_layout(a["w_out"][l]))
    w = _matmul_layout(a["w_in_2"][0])
    u, v, q, fg, iv, g, ga, gb = (w[8 * i:8 * i + 8] for i in range(8))
    for i in range(NT):
        for t in (fg, iv, q, g):
            put(t[i:i + 1])
    put(v)
    wb, wa = _matmul_layout(a["w_b_2"][0]), _matmul_layout(a["w_a_2"][0])
    for i in range(NT):
        put(gb[i:i + 1])
        put(wb[i:i + 1])
    put(u)
    for i in range(NT):
        put(ga[i:i + 1])
        put(wa[i:i + 1])
    put(_matmul_layout(a["w_o_2"][0]))
    put(a["w_ple_2"][0].reshape(2, P, 2, 4, P).transpose(2, 1, 3, 0, 4))
    put(_matmul_layout(a["w_ple_gate_2"][0]))
    wg, wu = _matmul_layout(a["w_ffn_gate_2"][0]), _matmul_layout(a["w_ffn_up_2"][0])
    wd = a["w_ffn_down_2"][0].reshape(FF // P, P, NT, P)
    at = 0
    for n in FF_GROUPS:
        for i in range(at, at + n):
            put(wg[i:i + 1])
            put(wu[i:i + 1])
        part = np.zeros((NT, P, NT, P), f)
        part[:, :, :n] = wd[at:at + n].transpose(2, 1, 0, 3)
        put(part)
        at += n
    stream = np.concatenate(slabs)
    assert stream.shape[0] == N_SLABS, stream.shape

    def cols(v):
        return v.reshape(-1, P).T

    def spread(v):
        return np.broadcast_to(v.reshape(1, -1), (P, v.size))

    vecs = np.stack([np.concatenate([
        cols(a["norm_g"][l]), cols(a["conv_b"][l]), cols(a["conv_ln_g"][l]), cols(a["conv_ln_b"][l]),
        a["conv_dw"][l].reshape(TAPS, NT, P).transpose(2, 1, 0).reshape(P, -1),
        cols(a["b_gate"][l]), cols(np.tile(a["q_norm_g"][l], 2)), cols(np.tile(a["k_norm_g"][l], 2)),
        spread(a["attn_sink"][l]), spread(a["ret_decay"][l])], 1) for l in range(DEPTH)])
    vec2 = np.concatenate([cols(a[n]) for n in (
        "ln0_g_2", "ln0_b_2", "b_in_2", "gm_norm_g_2", "gm_norm_b_2", "hg_lb_logits_2", "hg_norm_g_2",
        "ln1_g_2", "ln1_b_2", "ln2_g_2", "ln2_b_2", "b_ple_gate_2")], 1)

    pos = np.arange(T, dtype=f)

    def angles(theta, half):
        inv = f(theta) ** (-np.arange(half, dtype=f) / f(half))
        ang = pos[None, :] * inv[:, None]
        return np.cos(ang).astype(f), np.sin(ang).astype(f)

    cr, sr = angles(10000.0, P)
    ca, sa = angles(500000.0, 8)
    cos, sin = np.ones((P, T), f), np.zeros((P, T), f)
    rot = np.zeros((P, P), f)
    for h in (0, 64):
        for r in (0, 8):
            cos[h + r:h + r + 8], sin[h + r:h + r + 8] = ca, sa
        for r in range(8):
            rot[h + 8 + r, h + r] = -1.0
            rot[h + r, h + 8 + r] = 1.0
    part, col = np.arange(P)[:, None], np.arange(P)[None, :]
    bad = f(-1e30)
    amask = np.zeros((P, 3 * P), f)
    amask[:, 0:P] = np.where(col >= part, f(0), bad)
    amask[:, 2 * P:] = np.where(col <= part, f(0), bad)
    tab_hg = np.zeros((P, 2, T), f)
    tab_hg[:, 0] = (np.arange(T) % CHUNK16 != 0).astype(f)
    tab_hg[:, 1, 0:P] = ((part // CHUNK16 == col // CHUNK16) & (part <= col)).astype(f)
    for n, w in enumerate((32, 64, 128)):
        tab_hg[:, 1, (n + 1) * P:(n + 2) * P] = (
            (part // w == col // w) & (part % w < w // 2) & (col % w >= w // 2)).astype(f)
    arrays = {
        "slabs": stream, "vecs": vecs, "vec2": vec2,
        "x": a["x"][0].T.reshape(NT, P, T).transpose(1, 0, 2),
        "p": a["p_2"][0, 0].T.reshape(2, P, T).transpose(1, 0, 2),
        "gm_w": a["gm_w_s_2"][0].transpose(2, 0, 1),
        "gm_b": np.broadcast_to(a["gm_b_s_2"][0][None], (P, NT, P)),
        "ident": np.eye(P, dtype=f), "blk64": (part // 64 == col // 64).astype(f), "rot": rot, "amask": amask,
        "dist": (np.arange(896)[None, :] - part - 384).astype(np.int16),
        "tab_ret": np.stack([cr, sr], 1), "tab_att": np.stack([cos, sin], 1), "tab_hg": tab_hg,
    }
    arrays = {k: np.ascontiguousarray(v) for k, v in arrays.items()}
    nc = bacc.Bacc("TRN2", target_bir_lowering=False, num_devices=1)
    ins = {k: nc.dram_tensor(f"in_{k}", v.shape, mybir.dt.from_np(v.dtype), kind="ExternalInput").ap()
           for k, v in arrays.items()}
    out = nc.dram_tensor("out_y", (NT, P, T), mybir.dt.float32, kind="ExternalOutput").ap()
    xsave = nc.dram_tensor("xsave", (DEPTH + 1, P, NT, T), mybir.dt.float32, kind="Internal").ap()
    build(nc, ins, out, xsave)
    r = run_bass_kernel_spmd(nc, [{f"in_{k}": v for k, v in arrays.items()}], core_ids=[0])
    return r.results[0]["out_y"].reshape(D, T).T.reshape(1, T, D)
```
